# Optimizing a Trainium2 kernel written in Bass

```python
import jax, jax.numpy as jnp
from jax import lax
import numpy as np
import math

D_MODEL = 1024
BATCH = 1
SEQ = 256
DEPTH = 2

CHUNK = 64
HEAD_DIM = 128
MIX_WIDTH = D_MODEL
RET_WIDTH = MIX_WIDTH // 2
SB_WIDTH = MIX_WIDTH - RET_WIDTH
N_RET_HEADS = RET_WIDTH // HEAD_DIM
N_SB_HEADS = SB_WIDTH // HEAD_DIM
D_FF = ((8 * D_MODEL // 3 + 255) // 256) * 256
SB_BLOCK = 128
ROPE_BASE = 10000.0
EPS = 1e-6
IN_WIDTHS = (RET_WIDTH, RET_WIDTH, RET_WIDTH, RET_WIDTH, SB_WIDTH, SB_WIDTH, SB_WIDTH)
IN_WIDTH = sum(IN_WIDTHS)
IN_SPLITS = tuple(int(c) for c in np.cumsum(IN_WIDTHS)[:-1])


def rms_norm(x, g):
    xf = x.astype(jnp.float32)
    y = xf * lax.rsqrt(jnp.mean(xf * xf, axis=-1, keepdims=True) + EPS)
    return (y * g.astype(jnp.float32)).astype(x.dtype)

def to_heads(t, n_heads):
    b, s, _ = t.shape
    return t.reshape(b, s, n_heads, HEAD_DIM).transpose(0, 2, 1, 3)

def from_heads(t):
    b, h, s, d = t.shape
    return t.transpose(0, 2, 1, 3).reshape(b, s, h * d)

def head_group_norm(x, g):
    h, d = x.shape[1], x.shape[3]
    xf = x.astype(jnp.float32)
    mu = jnp.mean(xf, axis=-1, keepdims=True)
    var = jnp.mean(jnp.square(xf - mu), axis=-1, keepdims=True)
    y = (xf - mu) * lax.rsqrt(var + EPS) * g.astype(jnp.float32).reshape(h, 1, d)
    return y.astype(x.dtype)

def head_rms_norm(x, g):
    h, d = x.shape[1], x.shape[3]
    xf = x.astype(jnp.float32)
    y = xf * lax.rsqrt(jnp.mean(xf * xf, axis=-1, keepdims=True) + EPS)
    return (y * g.astype(jnp.float32).reshape(h, 1, d)).astype(x.dtype)

def apply_rotary(x):
    s, d = x.shape[2], x.shape[3]
    inv_freq = 1.0 / (ROPE_BASE ** (jnp.arange(0, d, 2, dtype=jnp.float32) / d))
    ang = jnp.arange(s, dtype=jnp.float32)[:, None] * inv_freq[None, :]
    cos = jnp.cos(ang).astype(x.dtype)
    sin = jnp.sin(ang).astype(x.dtype)
    x1, x2 = x[..., : d // 2], x[..., d // 2:]
    return jnp.concatenate([x1 * cos - x2 * sin, x1 * sin + x2 * cos], axis=-1)

def chunk_retention(q, k, v):
    b, h, s, d = q.shape
    c = CHUNK
    n = s // c
    dt = q.dtype
    log_g = jnp.log1p(-jnp.exp2(-5.0 - jnp.arange(h, dtype=jnp.float32)))
    i = jnp.arange(c, dtype=jnp.float32)
    intra_decay = jnp.exp(log_g[:, None, None] * jnp.abs(i[:, None] - i[None, :])).astype(dt)
    q_decay = jnp.exp(log_g[:, None] * (i + 1.0)).astype(dt)[..., None]
    k_decay = jnp.exp(log_g[:, None] * (c - 1.0 - i)).astype(dt)[..., None]
    chunk_decay = jnp.exp(log_g * c).astype(dt)[None, :, None, None]
    k = k * (d ** -0.5)
    qc = q.reshape(b, h, n, c, d)
    kc = k.reshape(b, h, n, c, d)
    vc = v.reshape(b, h, n, c, v.shape[-1])
    scores = jnp.einsum('bhnid,bhnjd->bhnij', qc, kc) * intra_decay[:, None]
    intra = jnp.einsum('bhnij,bhnje->bhnie', scores, vc)

    def step(state, inp):
        q_n, k_n, v_n = inp
        cross = jnp.einsum('bhid,bhde->bhie', q_n * q_decay, state)
        state = state * chunk_decay + jnp.einsum('bhjd,bhje->bhde', k_n * k_decay, v_n)
        return state, cross

    init = jnp.zeros((b, h, d, v.shape[-1]), dtype=intra.dtype)
    xs = (jnp.moveaxis(qc, 2, 0), jnp.moveaxis(kc, 2, 0), jnp.moveaxis(vc, 2, 0))
    _, cross = lax.scan(step, init, xs)
    out = intra + jnp.moveaxis(cross, 0, 2)
    return out.reshape(b, h, s, v.shape[-1])

def stick_breaking(q, k, v):
    s, d = q.shape[2], q.shape[3]
    scale = d ** -0.5
    outs = []
    for start in range(0, s, SB_BLOCK):
        end = start + SB_BLOCK
        qb = q[:, :, start:end]
        kb = k[:, :, :end]
        vb = v[:, :, :end]
        z = jnp.einsum('bhtd,bhsd->bhts', qb, kb).astype(jnp.float32) * scale
        t_pos = jnp.arange(start, end)[:, None]
        s_pos = jnp.arange(end)[None, :]
        valid = s_pos < t_pos
        log_keep = jnp.where(valid, jax.nn.log_sigmoid(-z), 0.0)
        later = lax.cumsum(log_keep, axis=3, reverse=True) - log_keep
        w = jnp.where(valid, jnp.exp(jax.nn.log_sigmoid(z) + later), 0.0)
        outs.append(jnp.einsum('bhts,bhse->bhte', w.astype(v.dtype), vb))
    return jnp.concatenate(outs, axis=2)

def first_inputs(seed: int = 0) -> dict:
    key = jax.random.key(seed)
    ks = jax.random.split(key, 12)
    f32 = jnp.float32

    def gain(k, shape):
        return (1.0 + 0.02 * jax.random.normal(k, shape, f32)).astype(f32)

    return {
        "x": jax.random.normal(ks[0], (BATCH, SEQ, D_MODEL), f32),
        "norm1_g": gain(ks[1], (DEPTH, D_MODEL)),
        "w_in": jax.random.normal(ks[2], (DEPTH, D_MODEL, IN_WIDTH), f32) * D_MODEL ** -0.5,
        "ret_norm_g": gain(ks[3], (DEPTH, RET_WIDTH)),
        "sb_norm_g": gain(ks[4], (DEPTH, SB_WIDTH)),
        "w_out": jax.random.normal(ks[5], (DEPTH, MIX_WIDTH, D_MODEL), f32) * MIX_WIDTH ** -0.5,
        "norm2_g": gain(ks[6], (DEPTH, D_MODEL)),
        "w_gate": jax.random.normal(ks[7], (DEPTH, D_MODEL, D_FF), f32) * D_MODEL ** -0.5,
        "w_up": jax.random.normal(ks[8], (DEPTH, D_MODEL, D_FF), f32) * D_MODEL ** -0.5,
        "w_down": jax.random.normal(ks[9], (DEPTH, D_FF, D_MODEL), f32) * D_FF ** -0.5,
        "final_g": gain(ks[10], (D_MODEL,)),
    }

def first_block(x, norm1_g, w_in, ret_norm_g, sb_norm_g, w_out, norm2_g, w_gate, w_up, w_down, final_g):
    for l in range(DEPTH):
        h = rms_norm(x, norm1_g[l])
        proj = h @ w_in[l]
        rq, rk, rv, rg, sq, sk, sv = jnp.split(proj, IN_SPLITS, axis=-1)
        ret = chunk_retention(apply_rotary(to_heads(rq, N_RET_HEADS)),
                              apply_rotary(to_heads(rk, N_RET_HEADS)),
                              to_heads(rv, N_RET_HEADS))
        ret = from_heads(head_group_norm(ret, ret_norm_g[l])) * jax.nn.silu(rg)
        sb = stick_breaking(to_heads(sq, N_SB_HEADS), to_heads(sk, N_SB_HEADS), to_heads(sv, N_SB_HEADS))
        sb = from_heads(head_rms_norm(sb, sb_norm_g[l]))
        x = x + jnp.concatenate([ret, sb], axis=-1) @ w_out[l]
        h = rms_norm(x, norm2_g[l])
        x = x + (jax.nn.silu(h @ w_gate[l]) * (h @ w_up[l])) @ w_down[l]
    return rms_norm(x, final_g)


GRID_W = 64
CTX_LEN = 256
N_MOD = 9
D_FF_2 = int(math.ceil(8 * D_MODEL / 3 / 128)) * 128
FFN_RES = 0.5
NEG_INF = -1e30

A_WIDTH = D_MODEL // 4
A_HEADS = 4
A_HEAD_DIM = A_WIDTH // A_HEADS
CHUNK_2 = 128
B_WIDTH = D_MODEL // 2
B_HEADS = 4
B_V_DIM = B_WIDTH // B_HEADS
B_QK_DIM = B_V_DIM // 2
C_WIDTH = D_MODEL // 4
C_HEAD_DIM = 64
C_HEADS = C_WIDTH // C_HEAD_DIM
C_KV_HEADS = 2
C_GROUP = C_HEADS // C_KV_HEADS
WINDOW = 128
BLK = 128
D_MIX = A_WIDTH + B_WIDTH + C_WIDTH

W_UV_A = 2 * A_WIDTH
W_Q_B = B_HEADS * 2 * B_QK_DIM
W_Q_C = C_HEADS * C_HEAD_DIM
W_K_B = B_HEADS * 2 * B_QK_DIM
W_V_B = B_HEADS * B_V_DIM
W_K_C = C_KV_HEADS * C_HEAD_DIM
W_V_C = C_KV_HEADS * C_HEAD_DIM
IN_COLS = W_UV_A + W_Q_B + W_Q_C + W_K_B + W_V_B + W_K_C + W_V_C
KV_START = W_UV_A + W_Q_B + W_Q_C
SPLITS = (W_UV_A, W_UV_A + W_Q_B, KV_START, KV_START + W_K_B, KV_START + W_K_B + W_V_B,
          KV_START + W_K_B + W_V_B + W_K_C)
KV_SPLITS = (W_K_B, W_K_B + W_V_B, W_K_B + W_V_B + W_K_C)


def rmsnorm(x, g):
    xf = x.astype(jnp.float32)
    y = xf * lax.rsqrt(jnp.mean(xf * xf, axis=-1, keepdims=True) + EPS)
    return (y * g.astype(jnp.float32)).astype(x.dtype)

def axial_rope_tables(rows, dim):
    row = jnp.repeat(jnp.arange(rows, dtype=jnp.float32), GRID_W)
    col = jnp.tile(jnp.arange(GRID_W, dtype=jnp.float32), rows)
    quarter = dim // 4
    inv = ROPE_BASE ** (-jnp.arange(quarter, dtype=jnp.float32) / quarter)
    ar = row[:, None] * inv[None, :]
    ac = col[:, None] * inv[None, :]
    ang = jnp.concatenate([ar, ar, ac, ac], axis=-1)
    return jnp.cos(ang), jnp.sin(ang)

def apply_rope(x, cos, sin):
    shape = (x.shape[1],) + (1,) * (x.ndim - 3) + (x.shape[-1],)
    cos = cos.reshape(shape).astype(x.dtype)
    sin = sin.reshape(shape).astype(x.dtype)
    x1, x2, x3, x4 = jnp.split(x, 4, axis=-1)
    rot = jnp.concatenate([-x2, x1, -x4, x3], axis=-1)
    return x * cos + rot * sin

def adaln_in(s, g_pre, shift, scale):
    return rmsnorm(s, g_pre) * (1 + scale) + shift

def adaln_out(s, y, g_post, gate, weight):
    return s + weight * gate * rmsnorm(y, g_post)

def swiglu(y, wg, wu, wd):
    return (jax.nn.silu(y @ wg) * (y @ wu)) @ wd

def ffn_sublayer(s, mod, j, g_pre, g_post, wg, wu, wd):
    y = adaln_in(s, g_pre, mod[..., 3 * j, :, :], mod[..., 3 * j + 1, :, :])
    return adaln_out(s, swiglu(y, wg, wu, wd), g_post, mod[..., 3 * j + 2, :, :], FFN_RES)

def chunk_gmlp(uv, v_gain, w_s, b_s):
    b_, l_, _ = uv.shape
    u, v = jnp.split(jax.nn.gelu(uv), 2, axis=-1)
    v = rmsnorm(v.reshape(b_, l_, A_HEADS, A_HEAD_DIM), v_gain)
    v = v.reshape(b_, l_ // CHUNK_2, CHUNK_2, A_HEADS, A_HEAD_DIM)
    mixed = jnp.einsum('hpq,bnqhc->bnphc', w_s, v) + b_s.T[:, :, None]
    return u * mixed.reshape(b_, l_, A_WIDTH)

def diff_softmax(q, k, v, lam):
    s = jnp.einsum('bqhmd,bkhmd->bhmqk', q, k).astype(jnp.float32) * (B_QK_DIM ** -0.5)
    p = jax.nn.softmax(s, axis=-1)
    w = p[:, :, 0] - lam * p[:, :, 1]
    return jnp.einsum('bhqk,bkhe->bqhe', w.astype(v.dtype), v)

def diff_attention_latent(q, k_all, v_all, lam):
    b_, l_ = q.shape[:2]
    nb = l_ // BLK
    qb = jnp.moveaxis(q.reshape((b_, nb, BLK) + q.shape[2:]), 1, 0)
    ob = lax.map(lambda qi: diff_softmax(qi, k_all, v_all, lam), qb)
    return jnp.moveaxis(ob, 0, 1).reshape((b_, l_) + ob.shape[3:])

def diff_post(o, g_sub, lam_init):
    return (rmsnorm(o, g_sub) * (1 - lam_init)).reshape(o.shape[0], o.shape[1], -1)

def swa_latent(q, k, v, kc, vc, sink):
    b_, l_ = q.shape[:2]
    nb = l_ // BLK
    qb = q.reshape(b_, nb, BLK, C_KV_HEADS, C_GROUP, C_HEAD_DIM)
    pad = ((0, 0), (1, 1), (0, 0), (0, 0), (0, 0))
    kp = jnp.pad(k.reshape(b_, nb, BLK, C_KV_HEADS, C_HEAD_DIM), pad)
    vp = jnp.pad(v.reshape(b_, nb, BLK, C_KV_HEADS, C_HEAD_DIM), pad)
    kband = jnp.concatenate([kp[:, :-2], kp[:, 1:-1], kp[:, 2:]], axis=2)
    vband = jnp.concatenate([vp[:, :-2], vp[:, 1:-1], vp[:, 2:]], axis=2)
    scale = C_HEAD_DIM ** -0.5
    s_band = jnp.einsum('bnqkgd,bnjkd->bnkgqj', qb, kband).astype(jnp.float32) * scale
    blk = jnp.arange(nb)
    qpos = blk[:, None] * BLK + jnp.arange(BLK)[None, :]
    kpos = (blk[:, None] - 1) * BLK + jnp.arange(3 * BLK)[None, :]
    valid = ((jnp.abs(qpos[:, :, None] - kpos[:, None, :]) <= WINDOW)
             & (kpos[:, None, :] >= 0) & (kpos[:, None, :] < l_))
    s_band = jnp.where(valid[None, :, None, None], s_band, NEG_INF)
    s_ctx = jnp.einsum('bnqkgd,bckd->bnkgqc', qb, kc).astype(jnp.float32) * scale
    s_sink = jnp.broadcast_to(sink.astype(jnp.float32)[None, None, :, :, None, None],
                              s_band.shape[:-1] + (1,))
    p = jax.nn.softmax(jnp.concatenate([s_band, s_ctx, s_sink], axis=-1), axis=-1)
    p_band = p[..., :3 * BLK].astype(v.dtype)
    p_ctx = p[..., 3 * BLK:-1].astype(v.dtype)
    out = (jnp.einsum('bnkgqj,bnjkd->bnqkgd', p_band, vband)
           + jnp.einsum('bnkgqc,bckd->bnqkgd', p_ctx, vc))
    return out.reshape(b_, l_, C_WIDTH)

def swa_context(q, kc, vc, sink):
    b_, l_ = q.shape[:2]
    s = jnp.einsum('bqkgd,bckd->bkgqc', q, kc).astype(jnp.float32) * (C_HEAD_DIM ** -0.5)
    s_sink = jnp.broadcast_to(sink.astype(jnp.float32)[None, :, :, None, None], s.shape[:-1] + (1,))
    p = jax.nn.softmax(jnp.concatenate([s, s_sink], axis=-1), axis=-1)[..., :-1]
    out = jnp.einsum('bkgqc,bckd->bqkgd', p.astype(vc.dtype), vc)
    return out.reshape(b_, l_, C_WIDTH)

def second_inputs(seed: int = 0) -> dict:
    key = jax.random.key(seed)
    ks = jax.random.split(key, 19)
    f32 = jnp.float32
    nrm = lambda k, shape, s: jax.random.normal(k, shape, f32) * s
    return {
        'x': nrm(ks[0], (BATCH, SEQ, D_MODEL), 1.0),
        'c': nrm(ks[1], (BATCH, D_MODEL), 1.0),
        'ctx': nrm(ks[2], (BATCH, CTX_LEN, D_MODEL), 1.0),
        'c_ctx': nrm(ks[3], (D_MODEL,), 1.0),
        'w_mod': nrm(ks[4], (DEPTH, D_MODEL, N_MOD * D_MODEL), 0.5 * D_MODEL ** -0.5),
        'b_mod': nrm(ks[5], (DEPTH, N_MOD * D_MODEL), 0.01),
        'norm_pre': 1.0 + nrm(ks[6], (DEPTH, 3, D_MODEL), 0.02),
        'norm_post': 1.0 + nrm(ks[7], (DEPTH, 3, D_MODEL), 0.02),
        'ffn_w_gate': nrm(ks[8], (DEPTH, 2, D_MODEL, D_FF_2), D_MODEL ** -0.5),
        'ffn_w_up': nrm(ks[9], (DEPTH, 2, D_MODEL, D_FF_2), D_MODEL ** -0.5),
        'ffn_w_down': nrm(ks[10], (DEPTH, 2, D_FF_2, D_MODEL), D_FF_2 ** -0.5),
        'w_in': nrm(ks[11], (DEPTH, D_MODEL, IN_COLS), D_MODEL ** -0.5),
        'w_out': nrm(ks[12], (DEPTH, D_MIX, D_MODEL), D_MIX ** -0.5),
        'gmlp_v_gain': 1.0 + nrm(ks[13], (DEPTH, A_HEADS, A_HEAD_DIM), 0.02),
        'gmlp_w_s': nrm(ks[14], (DEPTH, A_HEADS, CHUNK_2, CHUNK_2), CHUNK_2 ** -0.5),
        'gmlp_b_s': nrm(ks[15], (DEPTH, A_HEADS, CHUNK_2), 0.02),
        'diff_lambda': nrm(ks[16], (DEPTH, 4, B_QK_DIM), 0.1),
        'diff_subln': 1.0 + nrm(ks[17], (DEPTH, B_V_DIM), 0.02),
        'swa_sink': nrm(ks[18], (DEPTH, C_HEADS), 0.5),
    }

def second_block(x, c, ctx, c_ctx, w_mod, b_mod, norm_pre, norm_post, ffn_w_gate, ffn_w_up, ffn_w_down,
              w_in, w_out, gmlp_v_gain, gmlp_w_s, gmlp_b_s, diff_lambda, diff_subln, swa_sink):
    b_, l_, _ = x.shape
    c_len = ctx.shape[1]
    ROWS = l_ // GRID_W
    cos_b, sin_b = axial_rope_tables(ROWS, B_QK_DIM)
    cos_c, sin_c = axial_rope_tables(ROWS, C_HEAD_DIM)
    sc = jax.nn.silu(c)
    scc = jax.nn.silu(c_ctx)
    h = ctx
    for l in range(DEPTH):
        last = l == DEPTH - 1
        mod_x = (sc @ w_mod[l] + b_mod[l]).reshape(b_, N_MOD, 1, D_MODEL)
        mod_h = (scc @ w_mod[l] + b_mod[l]).reshape(N_MOD, 1, D_MODEL)
        lam_init = 0.8 - 0.6 * math.exp(-0.3 * l)
        lam_p = diff_lambda[l].astype(jnp.float32)
        lam = (jnp.exp(jnp.sum(lam_p[0] * lam_p[1])) - jnp.exp(jnp.sum(lam_p[2] * lam_p[3])) + lam_init)
        sink = swa_sink[l].reshape(C_KV_HEADS, C_GROUP)

        f0 = (norm_pre[l, 0], norm_post[l, 0], ffn_w_gate[l, 0], ffn_w_up[l, 0], ffn_w_down[l, 0])
        x = ffn_sublayer(x, mod_x, 0, *f0)
        h = ffn_sublayer(h, mod_h, 0, *f0)

        ax = adaln_in(x, norm_pre[l, 1], mod_x[:, 3], mod_x[:, 4])
        ah = adaln_in(h, norm_pre[l, 1], mod_h[3], mod_h[4])
        uv_x, qb_x, qc_x, kb_x, vb_x, kc_x, vc_x = jnp.split(ax @ w_in[l], SPLITS, axis=-1)
        if last:
            kb_h, vb_h, kc_h, vc_h = jnp.split(ah @ w_in[l][:, KV_START:], KV_SPLITS, axis=-1)
        else:
            uv_h, qb_h, qc_h, kb_h, vb_h, kc_h, vc_h = jnp.split(ah @ w_in[l], SPLITS, axis=-1)
        kb_h = kb_h.reshape(b_, c_len, B_HEADS, 2, B_QK_DIM)
        vb_h = vb_h.reshape(b_, c_len, B_HEADS, B_V_DIM)
        kc_h = kc_h.reshape(b_, c_len, C_KV_HEADS, C_HEAD_DIM)
        vc_h = vc_h.reshape(b_, c_len, C_KV_HEADS, C_HEAD_DIM)
        qb_x = apply_rope(qb_x.reshape(b_, l_, B_HEADS, 2, B_QK_DIM), cos_b, sin_b)
        kb_x = apply_rope(kb_x.reshape(b_, l_, B_HEADS, 2, B_QK_DIM), cos_b, sin_b)
        vb_x = vb_x.reshape(b_, l_, B_HEADS, B_V_DIM)
        qc_x = apply_rope(qc_x.reshape(b_, l_, C_KV_HEADS, C_GROUP, C_HEAD_DIM), cos_c, sin_c)
        kc_x = apply_rope(kc_x.reshape(b_, l_, C_KV_HEADS, C_HEAD_DIM), cos_c, sin_c)
        vc_x = vc_x.reshape(b_, l_, C_KV_HEADS, C_HEAD_DIM)

        o_a = chunk_gmlp(uv_x, gmlp_v_gain[l], gmlp_w_s[l], gmlp_b_s[l])
        k_all = jnp.concatenate([kb_h, kb_x], axis=1)
        v_all = jnp.concatenate([vb_h, vb_x], axis=1)
        o_b = diff_post(diff_attention_latent(qb_x, k_all, v_all, lam), diff_subln[l], lam_init)
        o_c = swa_latent(qc_x, kc_x, vc_x, kc_h, vc_h, sink)
        mix_x = jnp.concatenate([o_a, o_b, o_c], axis=-1) @ w_out[l]
        x = adaln_out(x, mix_x, norm_post[l, 1], mod_x[:, 5], 1.0)
        if not last:
            qb_h = qb_h.reshape(b_, c_len, B_HEADS, 2, B_QK_DIM)
            qc_h = qc_h.reshape(b_, c_len, C_KV_HEADS, C_GROUP, C_HEAD_DIM)
            oh_a = chunk_gmlp(uv_h, gmlp_v_gain[l], gmlp_w_s[l], gmlp_b_s[l])
            oh_b = diff_post(diff_softmax(qb_h, kb_h, vb_h, lam), diff_subln[l], lam_init)
            oh_c = swa_context(qc_h, kc_h, vc_h, sink)
            mix_h = jnp.concatenate([oh_a, oh_b, oh_c], axis=-1) @ w_out[l]
            h = adaln_out(h, mix_h, norm_post[l, 1], mod_h[5], 1.0)

        f1 = (norm_pre[l, 2], norm_post[l, 2], ffn_w_gate[l, 1], ffn_w_up[l, 1], ffn_w_down[l, 1])
        x = ffn_sublayer(x, mod_x, 2, *f1)
        if not last:
            h = ffn_sublayer(h, mod_h, 2, *f1)
    return x


def setup_inputs(seed=0):
    out = dict(first_inputs(seed))
    for name, value in second_inputs(seed + 1).items():
        if name != "x":
            out[name + "_2"] = value
    return out


def reference(
    x, norm1_g, w_in, ret_norm_g, sb_norm_g, w_out, norm2_g, w_gate, w_up, w_down, final_g, c_2,
    ctx_2, c_ctx_2, w_mod_2, b_mod_2, norm_pre_2, norm_post_2, ffn_w_gate_2, ffn_w_up_2,
    ffn_w_down_2, w_in_2, w_out_2, gmlp_v_gain_2, gmlp_w_s_2, gmlp_b_s_2, diff_lambda_2,
    diff_subln_2, swa_sink_2,
):
    x = first_block(
        x, norm1_g, w_in, ret_norm_g, sb_norm_g, w_out, norm2_g, w_gate, w_up, w_down, final_g,
    )
    return second_block(
        x, c_2, ctx_2, c_ctx_2, w_mod_2, b_mod_2, norm_pre_2, norm_post_2, ffn_w_gate_2,
        ffn_w_up_2, ffn_w_down_2, w_in_2, w_out_2, gmlp_v_gain_2, gmlp_w_s_2, gmlp_b_s_2,
        diff_lambda_2, diff_subln_2, swa_sink_2,
    )


_drawn_inputs = setup_inputs


def setup_inputs(seed=0):
    import zlib

    import numpy as np

    out = dict(_drawn_inputs(seed))
    spreads = {}
    factors = {'ret_norm_g': 5.776,
     'sb_norm_g': 3.325,
     'norm2_g': 3.087,
     'final_g': 2.813,
     'norm_pre_2': 4.546,
     'norm_post_2': 5.186,
     'gmlp_v_gain_2': 25.357,
     'gmlp_b_s_2': 73.425,
     'diff_subln_2': 200.0,
     'swa_sink_2': 8.0}
    for name, (base, spread) in spreads.items():
        noise = np.random.default_rng([zlib.crc32(name.encode()), seed]).standard_normal(out[name].shape)
        drawn = base * np.exp(spread * noise) if base else spread * noise
        out[name] = __import__('jax').numpy.asarray(drawn.astype(out[name].dtype))
    for name, factor in factors.items():
        out[name] = (out[name] * factor).astype(out[name].dtype)
    return out
```

```python
from collections import Counter
from contextlib import ExitStack
import math

import concourse.bass as bass
from concourse import mybir

F32 = mybir.dt.float32
F32R = mybir.dt.float32r
ALU = mybir.AluOpType
ACT = mybir.ActivationFunctionType
AX_X = mybir.AxisListType.X

P = 128
D = 1024
KD = D // P
F = 2816
KF = F // P
DEPTH = 2
EPS = 1e-6
BANK = 512
RING = 4
UNIT = 1024
CH = 512
WIN1_CHUNKS = 7
WIN2_CHUNKS = 5
GU_CHUNKS = F // 256
N_MOD = 9
MOD_CHUNKS = N_MOD * D // CH
HEADS = 8
NEG = -1e30
CHUNK = 64
GRID_W = 64
WINDOW = 128
ROPE_BASE = 10000.0
LAM_INIT = [0.8 - 0.6 * math.exp(-0.3 * l) for l in range(DEPTH)]

RQ, RK, RV, RG, SQ, SK, SV = (512 * i for i in range(7))
UV, QB, QC, KB, VB, KC, VC = 0, 512, 1024, 1280, 1792, 2304, 2432


def plan():
    subs = []
    for l in range(DEPTH):
        subs.append(dict(kind="ret", blk=1, l=l, tw=2, tt=2, chunks=WIN1_CHUNKS, k=KD, mod=True, norm=("n1", l)))
        subs.append(dict(kind="ffn", blk=1, l=l, tw=2, tt=2, chunks=GU_CHUNKS, k=KF, mod=True, norm=("n2", l)))
    for l in range(DEPTH):
        last = l == DEPTH - 1
        subs.append(dict(kind="ffn", blk=2, l=l, j=0, tw=4, tt=4, chunks=GU_CHUNKS, k=KF, mod=False))
        subs.append(dict(kind="mix", blk=2, l=l, j=1, tw=4, tt=2 if last else 4, chunks=WIN2_CHUNKS, k=KD, mod=False))
        t = 2 if last else 4
        subs.append(dict(kind="ffn", blk=2, l=l, j=2, tw=t, tt=t, chunks=GU_CHUNKS, k=KF, mod=False))
    unit = take = gate = mod = 0
    for s in subs:
        s["u_wide"] = unit
        unit += 4 * s["chunks"]
        s["u_tall"] = unit
        unit += s["k"]
        s["take0"] = take
        take += s["tw"] * s["chunks"]
        s["gate0"] = gate
        gate += s["tw"] * s["chunks"] * (s["kind"] == "ffn")
        s["mod0"] = mod
        mod += s["chunks"] * s["mod"]
    return subs, unit, mod


SUBS, N_UNITS, N_MODCH = plan()
LEAD = 4


def jobs_of(s):
    out = []
    for hg in range(6):
        for t in range(s["tt"]):
            if hg < 4:
                out.append(("B", hg, 0, t))
            else:
                out += [("C", hg, 0, t), ("C", hg, 1, t)]
    return out


def build(nc, a, out):
    ctx = ExitStack()
    with ctx:
        cursor = [max(nc.sbuf_base + 31, 16512) // 32 * 32]
        places = {}

        def at(name, shape, dt, offset):
            return nc.alloc_sbuf_tensor_at(name, shape, dt, offset=offset)

        def region(name, size):
            places[name] = cursor[0]
            cursor[0] += (size + 31) // 32 * 32
            assert cursor[0] <= nc.sbuf_usable_end, (name, cursor[0])
            return places[name]

        def sb(name, shape, dt=F32):
            return at(name, shape, dt, region(name, 4 * math.prod(shape[1:])))

        raw = sb("raw", [P, RING, UNIT])
        whi = sb("whi", [P, RING, UNIT], F32R)
        wlo = sb("wlo", [P, RING, UNIT], F32R)
        x = sb("x", [P, 4, D])
        ahi = sb("ahi", [P, 1024], F32R)
        alo = sb("alo", [P, 1024], F32R)
        rows = sb("rows", [P, 4, D])

        r_m = region("m", 16384)
        mraw = at("mraw", [P, RING, UNIT], F32, r_m)
        mixT2 = at("mixT2", [P, KD, 512], F32, r_m)
        diag2 = at("diag2", [P, 2, KD, P], F32, r_m)
        diag1 = at("diag1", [P, 1, KD, P], F32, places["rows"] + 8192)

        r_x = region("xs", 32768)
        xhi = at("xhi", [P, KD, 512], F32R, r_x)
        xlo = at("xlo", [P, KD, 512], F32R, r_x + 16384)
        qkT = at("qkT", [P, 2, 512], F32, r_x)
        wts = at("wts", [P, 4, 384], F32, r_x + 4096)
        zs = at("zs", [P, 2, 384], F32, r_x + 10240)
        es = at("es", [P, 2, 384], F32, r_x + 13312)
        rs_ = at("rsb", [P, 2, 384], F32, r_x + 16384)
        ls = at("ls", [P, 2, 384], F32, r_x + 19456)
        qT = at("qT", [P, 2, 512], F32, r_x)
        kT = at("kT", [P, 2, 512], F32, r_x + 4096)
        prob = at("prob", [P, 3, 2, 512], F32, r_x + 8192)
        wT = at("wT", [P, 2, 512], F32, r_x + 20480)
        ws = at("ws", [P, 4, P], F32, r_x + 24576)
        wmask = at("wmask", [P, 2, 256], F32, r_x + 30720)
        vsq = at("vsq", [P, 4, 256], F32, r_x + 26624)

        r_h = region("h", 45056)
        hid = at("hid", [P, KF, 512], F32, r_h)
        proj1 = at("proj1", [P, 2, 3584], F32, r_h)
        rope1 = at("rope1", [P, 2, D], F32, r_h + 28672)
        mixT1 = at("mixT1", [P, KD, 256], F32, r_h + 36864)
        proj2 = at("proj2", [P, 4, 2560], F32, r_h)
        rope2 = at("rope2", [P, 2, 512], F32, r_h + 40960)

        r_g = region("g", 8192)
        sgate = at("sgate", [P, 4, 256], F32, r_g)
        hrow = at("hrow", [P, 4, 256], F32, r_g + 4096)
        fbuf = at("fbuf", [P, 4, 256], F32, r_g + 4096)

        r_row = region("grow", 8192)
        grow = at("grow", [P, 2, D], F32, r_row)
        rmask = at("rmask", [P, 4, 384], F32, r_row)
        cs1 = at("cs1", [P, 2, 2, P], F32, r_row + 6144)

        ident = sb("ident", [P, P])
        ones = sb("ones", [P, P])
        tri = sb("tri", [P, P])
        future = sb("future", [P, 384])
        cs2 = sb("cs2", [P, 2, 2, 64])
        cols = sb("cols", [P, 15, KD])
        zero = sb("zero", [P, 1])
        bmod = sb("bmod", [P, DEPTH, N_MOD * KD])
        cT = sb("cT", [P, KD, 2])
        modT = sb("modT", [P, DEPTH, N_MOD * KD, 2])
        bcol = sb("bcol", [P, DEPTH, 4])
        acol = sb("acol", [P, 2, KD])
        gcol = sb("gcol", [P, 2, KD])
        mixcol = sb("mixcol", [P, KD])
        vgain = sb("vgain", [P, DEPTH, 256])
        lamw = at("lamw", [P, DEPTH, 4, 64], F32, places["rows"])
        lprod = at("lprod", [P, DEPTH, 2, 64], F32, places["rows"] + 4096)
        lsum = sb("lsum", [P, DEPTH, 2])
        nlam = sb("nlam", [P, DEPTH])
        sink = sb("sink", [P, DEPTH, 4])
        nsink = sb("nsink", [P, DEPTH, 4])
        sq = sb("sq", [P, 4])
        ms = sb("ms", [P, 16])
        rstd = sb("rstd", [P, 16])
        mhalf = sb("mhalf", [P, 16])
        stats = sb("stats", [P, 16, 6])
        mv = sb("mv", [P, 16, 2])
        mx = sb("mx", [P, 2, 2])
        nb = sb("nb", [P, 3, 2])
        den = sb("den", [P, 3, 2])
        esink = sb("esink", [P, 3])
        rden = sb("rden", [P, 2])

        ps = ctx.enter_context(nc.psum_tensor("ps", [P, 8 * BANK], F32))

        def bank(b, lo=0, hi=BANK):
            return ps[:, BANK * b + lo:BANK * b + hi]

        def sem(name):
            return ctx.enter_context(nc.semaphore(name))

        consts_landed = sem("consts_landed")
        x_landed = sem("x_landed")
        raw_landed = [sem(f"raw_landed{i}") for i in range(RING)]
        mraw_landed = [sem(f"mraw_landed{i}") for i in range(RING)]
        ws_landed = sem("ws_landed")
        out_landed = sem("out_landed")
        hi_done = sem("hi_done")
        w_split = sem("w_split")
        w_used = sem("w_used")
        mod_used = sem("mod_used")
        mod_taken = sem("mod_taken")
        chunk_taken = sem("chunk_taken")
        silu_done = sem("silu_done")
        gate_done = sem("gate_done")
        hT_done = sem("hT_done")
        c_silu = sem("c_silu")
        sq_done = sem("sq_done")
        ms_ready = sem("ms_ready")
        rstd_ready = sem("rstd_ready")
        xn_ready = sem("xn_ready")
        tr_ready = sem("tr_ready")
        f_ready = sem("f_ready")
        xhi_ready = sem("xhi_ready")
        xs_ready = sem("xs_ready")
        y_ready = sem("y_ready")
        x_ready = sem("x_ready")
        cols_ready = sem("cols_ready")
        diag_ready = sem("diag_ready")
        g_ready = sem("g_ready")
        grow_ready = sem("grow_ready")
        dve_link = sem("dve_link")
        act_link = sem("act_link")
        pool_link = sem("pool_link")
        lam_ready = sem("lam_ready")
        lexp_ready = sem("lexp_ready")
        rope_done = sem("rope_done")
        rg_done = sem("rg_done")
        gelu_done = sem("gelu_done")
        qkT_ready = sem("qkT_ready")
        qkT_copied = sem("qkT_copied")
        z_ready = sem("z_ready")
        z_taken = sem("z_taken")
        z_scaled = sem("z_scaled")
        l_ready = sem("l_ready")
        lm_ready = sem("lm_ready")
        s_ready = sem("s_ready")
        w_ready = sem("w_ready")
        v_ready = sem("v_ready")
        o_copied = sem("o_copied")
        v_scaled = sem("v_scaled")
        mixed_ready = sem("mixed_ready")
        max_ready = sem("max_ready")
        exp_ready = sem("exp_ready")
        prob_ready = sem("prob_ready")
        wT_ready = sem("wT_ready")
        wT_copied = sem("wT_copied")
        mix_ready = sem("mix_ready")
        mixT_dve = sem("mixT_dve")
        mixT_act = sem("mixT_act")

        n_consts = 15
        block = ctx.enter_context(nc.Block())

        def c_n1(l):
            return l

        def c_n2(l):
            return 2 + l

        def c_mix1(l):
            return 4 + l

        C_FINAL = 6

        def c_pre(l, j):
            return 7 + 3 * l + j

        post = sb("post", [P, 6, KD])

        def c_post(l, j):
            return 3 * l + j

        def rows_wanted(s):
            if s["blk"] == 2:
                return s["tt"] // 2, s["tw"] if s["tw"] == 4 else 4, diag2
            if s["kind"] == "ffn" and s["l"] == DEPTH - 1:
                return 1, 6, diag1
            return 0, 0, None

        def pair_bank(s, pair, st):
            return 4 + pair if s["tw"] == 2 else 4 + (2 * pair + st) % 4

        def taken_total(s):
            return LEAD + s["take0"] + s["tw"] * s["chunks"]

        @block.sync
        def _(sp):
            def load_main(u, slot, first=False):
                if not first:
                    sp.wait_ge(w_split, u - RING + 1)
                sp.dma_start(raw[:, slot, :], a["w"][u]).then_inc(raw_landed[slot], 16)

            def load_mod(m, slot):
                sp.wait_ge(mod_used, m + 1)
                sp.dma_start(mraw[:, slot, :], a["w_mod"][m]).then_inc(mraw_landed[slot], 16)

            sp.dma_start(x[:, 0:2, :], a["x"].rearrange("b (t p) d -> p (b t) d", p=P)).then_inc(x_landed, 16)
            for name, dst in (("ident", ident), ("cs1", cs1), ("cols", cols), ("cT", cT), ("tri", tri),
                              ("future", future), ("rmask", rmask), ("bmod", bmod), ("cs2", cs2), ("post", post), ("bcol", bcol)):
                sp.dma_start(dst[tuple([slice(None)] * len(dst.shape))], a[name]).then_inc(consts_landed, 16)
            for name, dst in (("lam", lamw), ("sink", sink), ("vgain", vgain)):
                sp.dma_start(dst[tuple([slice(None)] * len(dst.shape))],
                             a[name].partition_broadcast(P)).then_inc(consts_landed, 16)
            sp.dma_start(x[:, 2:4, :], a["ctx"].rearrange("b (t p) d -> p (b t) d", p=P)).then_inc(consts_landed, 16)
            for s in SUBS:
                for c in range(1 if s["mod"] and s["u_wide"] == 0 else 0):
                    for u in range(4):
                        load_main(u, u, first=True)
                        load_mod(u, u)
                done = 1 if s["u_wide"] == 0 else 0
                with sp.Fori(0, s["chunks"] - done) as i:
                    for u in range(4):
                        unit = s["u_wide"] + 4 * done + u
                        load_main(4 * i + unit, unit % RING)
                        if s["mod"]:
                            load_mod(4 * i + (4 * s["mod0"] + 4 * done + u), u)
                loops = s["k"] // 4
                with sp.Fori(0, loops) as i:
                    for u in range(4):
                        unit = s["u_tall"] + u
                        load_main(4 * i + unit, unit % RING)
                for u in range(4 * loops, s["k"]):
                    unit = s["u_tall"] + u
                    load_main(unit, unit % RING)
            sp.wait_ge(x_ready, sum(s["tt"] for s in SUBS) + 2)
            sp.dma_start(out.rearrange("b (t p) d -> p (b t) d", p=P), x[:, 0:2, :]).then_inc(out_landed, 16)
            sp.wait_ge(out_landed, 16)

        def wide_loop(eng, s, body):
            body(0, 0, True)
            with eng.Fori(0, (s["chunks"] - 1) // 2) as i:
                body(2 * i + 1, 1, False)
                body(2 * i + 2, 0, False)

        def tall_loop(eng, s, body, done=0):
            loops = (s["k"] - 1) // 4
            for k in range(done, 4):
                body(k, k, 0, False)
            if loops > 1:
                with eng.Fori(1, loops) as i:
                    for j in range(4):
                        body(4 * i + j, j, i, False)
            for k in range(4 * loops, s["k"]):
                body(k, k % 4, k // 4, k == s["k"] - 1)

        @block.tensor
        def _(pe):
            n = Counter()
            pe.sem_inc(w_used, LEAD)
            pe.sem_inc(mod_used, LEAD)
            pe.sem_inc(hT_done, LEAD)

            def mm(o, lhsT, rhs, start, stop):
                return nc.tensor.matmul(o, lhsT, rhs, start=start, stop=stop, skip_group_check=True)

            def transpose_pair(s, pair):
                streams = s["tw"] // 2
                for st in range(streams):
                    pe.wait_ge(xn_ready, n["xn"] + 2 * (st + 1))
                    if streams == 2 and pair >= 2:
                        pe.wait_ge(f_ready, n["xs"] + streams * (2 * pair - 3) + st + 1)
                    for kk in range(2):
                        for t in range(2):
                            o = bank(pair_bank(s, pair, st), 256 * kk + 128 * t, 256 * kk + 128 * t + 128)
                            last = nc.tensor.transpose(o, rows[:, 2 * st + t, P * (2 * pair + kk):P * (2 * pair + kk + 1)],
                                                       ident[:, :])
                    last.then_inc(tr_ready, 1)

            def broadcast_rows(s):
                streams, first_bank, diag = rows_wanted(s)
                if not streams:
                    return
                pe.wait_ge(chunk_taken, taken_total(s) - s["tw"])
                for st in range(streams):
                    pe.wait_ge(diag_ready, n["diag"] + st + 1)
                    for k in range(KD):
                        last = mm(bank(first_bank + 2 * st + k // 4, P * (k % 4), P * (k % 4) + P),
                                  ones[:, :], diag[:, st, k, :], True, True)
                    last.then_inc(g_ready, 1)
                n["diag"] += streams

            def wide(s):
                tw = s["tw"]
                streams = tw // 2
                for pair in range(4 if streams == 1 else 2):
                    transpose_pair(s, pair)

                def gate_transposes(c, par):
                    for t in range(tw):
                        pe.wait_ge(gate_done, LEAD + s["gate0"] + tw * c + (t + 1))
                        for h in range(2):
                            last = nc.tensor.transpose(bank(tw * par + t, P * h, P * h + P),
                                                       hrow[:, t, P * h:P * h + P], ident[:, :])
                        last.then_inc(hT_done, 1)

                def chunk(c, par, first):
                    for u in range(4):
                        slot = (s["u_wide"] + u) % RING
                        pe.wait_ge(w_split, s["u_wide"] + u + 1 + 4 * c)
                        if first:
                            pe.wait_ge(xs_ready, n["xs"] + streams * (2 * u + 2))
                        if u == 0:
                            pe.wait_ge(chunk_taken, LEAD + s["take0"] - tw + tw * c)
                        for kk in range(2):
                            k = 2 * u + kk
                            hi, lo = (w[:, slot, CH * kk:CH * kk + CH] for w in (whi, wlo))
                            for t in range(tw):
                                o = bank(tw * par + t)
                                xh, xl = (v[:, k, P * t:P * t + P] for v in (xhi, xlo))
                                mm(o, xh, hi, k == 0, False)
                                mm(o, xh, lo, False, False)
                                last = mm(o, xl, hi, False, k == KD - 1)
                        last.then_inc(w_used, 1)
                        if s["mod"]:
                            pe.wait_ge(mraw_landed[u], 16 * (s["mod0"] + 1) + 16 * c)
                            if u == 0:
                                pe.wait_ge(mod_taken, s["mod0"] + 1 + c)
                                if first and s["mod0"] == 0:
                                    pe.wait_ge(c_silu, 1)
                            for kk in range(2):
                                for nt in range(4):
                                    last = mm(bank(4, 2 * nt, 2 * nt + 2),
                                              mraw[:, u, CH * kk + P * nt:CH * kk + P * nt + P],
                                              cT[:, 2 * u + kk, :], u == kk == nt == 0, u == 3 and kk == 1)
                            last.then_inc(mod_used, 1)
                        if first and streams == 2 and u < 2:
                            transpose_pair(s, u + 2)
                        if u == 1 and not first and s["kind"] == "ffn":
                            gate_transposes(c - 1, 1 - par)

                wide_loop(pe, s, chunk)
                n["xs"] += KD * streams
                n["xn"] += tw
                broadcast_rows(s)
                if s["kind"] == "ffn":
                    gate_transposes(s["chunks"] - 1, 0)

            def tall(s):
                tt = s["tt"]
                pe.wait_ge(chunk_taken, taken_total(s))

                def unit(k, j, i, final):
                    slot = (s["u_tall"] + j) % RING
                    pe.wait_ge(w_split, s["u_tall"] + 1 + k)
                    aslot = j % (RING if tt == 2 else 2)
                    for t in range(tt):
                        ah, al = (v[:, P * tt * aslot + P * t:P * tt * aslot + P * t + P] for v in (ahi, alo))
                        for h in range(2):
                            hi, lo = (w[:, slot, CH * h:CH * h + CH] for w in (whi, wlo))
                            o = bank(2 * t + h)
                            mm(o, ah, hi, isinstance(k, int) and k == 0, False)
                            mm(o, ah, lo, False, False)
                            last = mm(o, al, hi, False, final)
                        if final and t < tt - 1:
                            last.then_inc(y_ready, 1)
                    last.then_inc(w_used, 1)

                tall_loop(pe, s, unit)

            def retention_and_stick(s):
                l = s["l"]
                pe.wait_ge(chunk_taken, taken_total(s))
                pe.wait_ge(rope_done, 2 * (l + 1))

                def transposes(h):
                    g = 8 * l + h
                    if h >= 2:
                        pe.wait_ge(qkT_copied, g - 1)
                    q0, k0 = (RQ + P * h, RK + P * h) if h < 4 else (SQ + P * (h - 4), SK + P * (h - 4))
                    for i, c0 in enumerate((q0, k0)):
                        for t in range(2):
                            last = nc.tensor.transpose(bank(h % 2, 256 * i + P * t, 256 * i + P * t + P),
                                                       proj1[:, t, c0:c0 + P], ident[:, :])
                    last.then_inc(qkT_ready, 1)

                def scores(h):
                    g = 8 * l + h
                    pe.wait_ge(qkT_copied, g + 1)
                    if h >= 2:
                        pe.wait_ge(z_taken, g - 1)
                    b, s_ = 2 + h % 2, h % 2
                    mm(bank(b, 0, 256), qkT[:, s_, 256:384], qkT[:, s_, 0:256], True, True)
                    mm(bank(b, 256, 384), qkT[:, s_, 384:512], qkT[:, s_, 128:256], True, True).then_inc(z_ready, 1)

                def suffix_sums(h):
                    pe.wait_ge(lm_ready, 4 * l + h - 4 + 1)
                    b, s_ = 2 + h % 2, h % 2
                    mm(bank(b, 0, 256), tri[:, :], ls[:, s_, 0:256], True, False)
                    mm(bank(b, 128, 256), ones[:, :], ls[:, s_, 256:384], False, True)
                    mm(bank(b, 256, 384), tri[:, :], ls[:, s_, 256:384], True, True).then_inc(s_ready, 1)

                def values(h):
                    g = 8 * l + h
                    if h < 4:
                        pe.wait_ge(z_taken, g + 1)
                    else:
                        pe.wait_ge(w_ready, 4 * l + h - 4 + 1)
                    if h >= 2:
                        pe.wait_ge(o_copied, g - 1)
                    c0 = RV + P * h if h < 4 else SV + P * (h - 4)
                    w, b = wts[:, h % 4, :], 4 + h % 2
                    mm(bank(b, 0, P), w[:, 0:P], proj1[:, 0, c0:c0 + P], True, True)
                    mm(bank(b, P, 2 * P), w[:, P:2 * P], proj1[:, 0, c0:c0 + P], True, False)
                    mm(bank(b, P, 2 * P), w[:, 2 * P:3 * P], proj1[:, 1, c0:c0 + P], False, True).then_inc(v_ready, 1)

                for i in range(HEADS + 3):
                    if i < HEADS:
                        transposes(i)
                    if 0 <= i - 1 < HEADS:
                        scores(i - 1)
                    if 4 <= i - 2 < HEADS:
                        suffix_sums(i - 2)
                    if 0 <= i - 3 < HEADS:
                        values(i - 3)
                mix_transposes(s)

            def mix_transposes(s):
                for st in range(s["tt"] // 2):
                    pe.wait_ge(mix_ready, n["mix"] + 2 * (st + 1))
                    for pair in range(4):
                        for kk in range(2):
                            for t in range(2):
                                o = bank(4 * st + pair, 256 * kk + 128 * t, 256 * kk + 128 * t + 128)
                                last = nc.tensor.transpose(o, rows[:, 2 * st + t, P * (2 * pair + kk):P * (2 * pair + kk + 1)],
                                                           ident[:, :])
                        last.then_inc(tr_ready, 1)
                n["mix"] += s["tt"]
                pe.wait_ge(mixT_dve, n["mixT"] + s["tt"])
                pe.wait_ge(mixT_act, n["mixT"] + s["tt"])
                n["mixT"] += s["tt"]

            def mixer2(s):
                l = s["l"]
                jobs = jobs_of(s)
                pe.wait_ge(chunk_taken, taken_total(s))
                pe.wait_ge(ws_landed, 32 * (l + 1))
                for t in range(s["tt"]):
                    pe.wait_ge(v_scaled, n["vs"] + t + 1)
                    for h in range(4):
                        last = mm(bank(t, 64 * h, 64 * h + 64), ws[:, h, :],
                                  proj2[:, t, 256 + 64 * h:256 + 64 * h + 64], True, True)
                    last.then_inc(mixed_ready, 1)
                n["vs"] += s["tt"]
                pe.wait_ge(rope_done, 2 * DEPTH + 8 * (l + 1))

                def transposes(hg):
                    hgg = n["hg"] + hg
                    q0 = QB + P * hg if hg < 4 else QC + P * (hg - 4)
                    k0 = KB + P * hg if hg < 4 else KC
                    if hgg >= 1:
                        pe.wait_ge(qkT_copied, HEADS * DEPTH + hgg)
                    for b, c0, tiles in ((4, q0, s["tt"]), (5, k0, 4)):
                        for t in range(tiles):
                            last = nc.tensor.transpose(bank(b, P * t, P * t + P), proj2[:, t, c0:c0 + P], ident[:, :])
                    last.then_inc(qkT_ready, 1)

                def scores(j):
                    kind, hg, m, t = jobs[j]
                    g = n["job"] + j
                    pe.wait_ge(qkT_copied, HEADS * DEPTH + n["hg"] + hg + 1)
                    if j >= 2:
                        pe.wait_ge(exp_ready, g - 1)
                    elif j == 0:
                        pe.wait_ge(o_copied, HEADS * DEPTH + n["job"] + n["oa"] + s["tt"])
                    keys = (0, 512) if t < 2 else (256, 512)
                    for i, mm_ in enumerate((0, 1) if kind == "B" else (m,)):
                        part = slice(64 * mm_, 64 * mm_ + 64)
                        last = mm(bank(2 * (j % 2) + i, 0, keys[1] - keys[0]), qT[part, hg % 2, P * t:P * t + P],
                                  kT[part, hg % 2, keys[0]:keys[1]], True, True)
                    last.then_inc(z_ready, 1)

                def prob_transposes(j):
                    kind, hg, m, t = jobs[j]
                    g = n["job"] + j
                    pe.wait_ge(prob_ready, g + 1)
                    if g >= 1:
                        pe.wait_ge(wT_copied, g)
                    for i in range(4 if t < 2 else 2):
                        last = nc.tensor.transpose(bank(6, P * i, P * i + P), prob[:, j % 3, 0, P * i:P * i + P], ident[:, :])
                    last.then_inc(wT_ready, 1)

                def values(j):
                    kind, hg, m, t = jobs[j]
                    g = n["job"] + j
                    pe.wait_ge(wT_copied, g + 1)
                    pe.wait_ge(o_copied, HEADS * DEPTH + g + n["oa"] + s["tt"])
                    c0, width = (VB + P * hg, P) if kind == "B" else (VC + 64 * m, 64)
                    tiles = (0, 1, 2, 3) if t < 2 else (2, 3)
                    for i, kt in enumerate(tiles):
                        last = mm(bank(7, 0, width), wT[:, j % 2, P * i:P * i + P], proj2[:, kt, c0:c0 + width],
                                  i == 0, i == len(tiles) - 1)
                    last.then_inc(v_ready, 1)

                transposes(0)
                for j in range(len(jobs) + 3):
                    if j < len(jobs):
                        hg = jobs[j][1]
                        if (j == 0 or jobs[j - 1][1] != hg) and hg < 5:
                            transposes(hg + 1)
                        scores(j)
                    if 0 <= j - 2 < len(jobs):
                        prob_transposes(j - 2)
                    if 0 <= j - 3 < len(jobs):
                        values(j - 3)
                n["job"] += len(jobs)
                n["oa"] += s["tt"]
                n["hg"] += 6
                mix_transposes(s)

            pe.wait_ge(consts_landed, 16 * n_consts)
            for i, s in enumerate(SUBS):
                if i:
                    if i == 2 * DEPTH:
                        n["x"] += 2
                    pe.wait_ge(x_ready, n["x"])
                wide(s)
                if s["kind"] == "ret":
                    retention_and_stick(s)
                if s["kind"] == "mix":
                    mixer2(s)
                tall(s)
                n["x"] += s["tt"]

        @block.scalar
        def _(act):
            n = Counter()
            act.sem_inc(chunk_taken, LEAD)

            def link(ins):
                n["link"] += 1
                ins.then_inc(act_link, 1)
                act.wait_ge(act_link, n["link"])

            def split_hi(s, key, j, i):
                u = s[key] + j
                slot = u % RING
                act.wait_ge(w_used, u + 1 + 4 * i)
                act.wait_ge(raw_landed[slot], 16 * (u // RING + 1) + 16 * i)
                nc.scalar.copy(whi[:, slot, :], raw[:, slot, :]).then_inc(hi_done, 1)

            def split_rows(tiles):
                for k in range(KD):
                    for st in range(tiles // 2):
                        act.wait_ge(f_ready, n["f"] + 1)
                        nc.scalar.copy(xhi[:, k, 256 * st:256 * st + 256], fbuf[:, n["f"] % 4, :]).then_inc(xhi_ready, 1)
                        n["f"] += 1

            def wide(s):
                tw = s["tw"]

                def silus(c, par):
                    for t in range(tw):
                        if t == 0:
                            act.wait_ge(w_used, LEAD + s["u_wide"] + 4 + 4 * c)
                        act.wait_ge(gate_done, LEAD + s["gate0"] - tw + t + 1 + tw * c)
                        nc.scalar.activation(sgate[:, t, :], bank(tw * par + t, 0, 256), ACT.Silu).then_inc(silu_done, 1)

                def hidden_out(c, par):
                    for t in range(tw):
                        act.wait_ge(hT_done, LEAD + s["gate0"] + t + 1 + tw * c)
                        src = bank(tw * par + t, 0, 256).rearrange("p (k c) -> p k c", k=2)
                        nc.scalar.copy(hid[:, bass.ds(2 * c, 2), P * t:P * t + P], src).then_inc(chunk_taken, 1)

                def proj_out(c, par):
                    dst = proj1 if s["kind"] == "ret" else proj2
                    for t in range(tw):
                        if t == 0:
                            act.wait_ge(w_used, LEAD + s["u_wide"] + 4 + 4 * c)
                        nc.scalar.copy(dst[:, t, bass.ds(CH * c, CH)], bank(tw * par + t)).then_inc(chunk_taken, 1)

                def chunk(c, par, first):
                    if first:
                        return
                    split_hi(s, "u_wide", 0, c)
                    split_hi(s, "u_wide", 1, c)
                    if not first:
                        if s["kind"] == "ffn":
                            silus(c - 1, 1 - par)
                        else:
                            proj_out(c - 1, 1 - par)
                    split_hi(s, "u_wide", 2, c)
                    split_hi(s, "u_wide", 3, c)
                    if not first and s["kind"] == "ffn":
                        hidden_out(c - 1, 1 - par)

                wide_loop(act, s, chunk)
                c = s["chunks"] - 1
                if s["kind"] == "ffn":
                    tall_first(s)
                    silus(c, 0)
                    grow_out(s)
                    hidden_out(c, 0)
                else:
                    grow_out(s)
                    proj_out(c, 0)

            def tall_unit(s):
                tt = s["tt"]
                src = hid if s["kind"] == "ffn" else (mixT1 if s["kind"] == "ret" else mixT2)
                aring = RING if tt == 2 else 2

                def unit(k, j, i, final):
                    aslot = j % aring
                    act.wait_ge(w_used, LEAD + s["u_tall"] - aring + 1 + k)
                    w = P * tt
                    nc.scalar.copy(ahi[:, w * aslot:w * aslot + w], src[:, k, 0:w] if isinstance(k, int)
                                   else src[:, bass.ds(k, 1), 0:w])
                    split_hi(s, "u_tall", j, i)

                return unit

            def tall_first(s):
                act.wait_ge(chunk_taken, taken_total(s) - s["tw"])
                for k in range(2):
                    tall_unit(s)(k, k, 0, False)

            def tall(s):
                if s["kind"] != "ffn":
                    act.wait_ge(mixT_dve, n["mixT"])
                    act.wait_ge(mixT_act, n["mixT"])
                else:
                    act.wait_ge(chunk_taken, taken_total(s))
                tall_loop(act, s, tall_unit(s), 2 if s["kind"] == "ffn" else 0)

            def retention_and_stick(s):
                l = s["l"]
                for t in range(2):
                    nc.scalar.activation(proj1[:, t, RG:RG + 512], proj1[:, t, RG:RG + 512], ACT.Silu).then_inc(rg_done, 1)
                for i in range(HEADS + 3):
                    if i < HEADS:
                        h, g = i, 8 * l + i
                        act.wait_ge(qkT_ready, g + 1)
                        if h >= 2:
                            act.wait_ge(z_ready, g - 1)
                        nc.scalar.copy(qkT[:, h % 2, :], bank(h % 2)).then_inc(qkT_copied, 1)
                    if 4 <= i - 1 < HEADS:
                        h = i - 1
                        gs = 4 * l + h - 4
                        act.wait_ge(z_scaled, gs + 1)
                        if h >= 6:
                            act.wait_ge(lm_ready, gs - 1)
                        e = es[:, h % 2, :]
                        link(nc.scalar.activation(e, zs[:, h % 2, :], ACT.Abs))
                        link(nc.scalar.activation(e, e, ACT.Exp, scale=-1.0))
                        nc.scalar.activation(e, e, ACT.Ln, bias=1.0).then_inc(l_ready, 1)
                    if 4 <= i - 2 < HEADS:
                        h, g = i - 2, 8 * l + i - 2
                        act.wait_ge(z_taken, g + 1)
                        act.wait_ge(v_ready, g - 3)
                        nc.scalar.activation(wts[:, h % 4, :], zs[:, h % 2, :], ACT.Exp).then_inc(w_ready, 1)
                    if 0 <= i - 3 < HEADS:
                        h, g = i - 3, 8 * l + i - 3
                        act.wait_ge(v_ready, g + 1)
                        nc.scalar.copy(rows[:, 0:2, P * h:P * h + P],
                                       bank(4 + h % 2, 0, 256).rearrange("p (t c) -> p t c", t=2)).then_inc(o_copied, 1)
                mix_out(s, mixT1)

            def mix_out(s, dst):
                for st in range(s["tt"] // 2):
                    for pair in (1, 3):
                        act.wait_ge(tr_ready, n["tr"] + 4 * st + pair + 1)
                        for kk in range(2):
                            k = 2 * pair + kk
                            col = cols[:, c_mix1(s["l"]), k:k + 1] if s["kind"] == "ret" else mixcol[:, k:k + 1]
                            last = nc.scalar.activation(dst[:, k, 256 * st:256 * st + 256],
                                                        bank(4 * st + pair, 256 * kk, 256 * kk + 256), ACT.Copy, scale=col)
                        last.then_inc(mixT_act, 1)
                    pass
                n["tr"] += 2 * s["tt"]
                n["mixT"] += s["tt"]

            def mixer2(s):
                l = s["l"]
                jobs = jobs_of(s)
                scale = 64 ** -0.5
                for t in range(s["tt"]):
                    nc.scalar.activation(proj2[:, t, 0:512], proj2[:, t, 0:512], ACT.Gelu_apprx_tanh).then_inc(gelu_done, 1)

                def qk_copy(hg):
                    hgg = n["hg"] + hg
                    act.wait_ge(qkT_ready, HEADS * DEPTH + hgg + 1)
                    nc.scalar.copy(qT[:, hg % 2, 0:P * s["tt"]], bank(4, 0, P * s["tt"]))
                    nc.scalar.copy(kT[:, hg % 2, :], bank(5)).then_inc(qkT_copied, 1)

                qk_copy(0)
                for j in range(len(jobs) + 3):
                    if j < len(jobs):
                        kind, hg, m, t = jobs[j]
                        g = n["job"] + j
                        if (j == 0 or jobs[j - 1][1] != hg) and hg < 5:
                            qk_copy(hg + 1)
                        act.wait_ge(max_ready, g + 1)
                        if g >= 3:
                            act.wait_ge(wT_ready, g - 2)
                        w = 512 if t < 2 else 256
                        b, slot = 2 * (j % 2), j % 3
                        for i in range(2 if kind == "B" else 1):
                            last = nc.scalar.activation(prob[:, slot, i, 0:w], bank(b + i, 0, w), ACT.Exp,
                                                        bias=nb[:, slot, i:i + 1], scale=scale, accum_out=den[:, slot, i:i + 1])
                        if kind == "C":
                            head = 2 * m + (hg - 4)
                            last = nc.scalar.activation(esink[:, slot:slot + 1], sink[:, l, head:head + 1], ACT.Exp,
                                                        bias=nb[:, slot, 0:1])
                        last.then_inc(exp_ready, 1)
                    if 0 <= j - 2 < len(jobs):
                        kind, hg, m, t = jobs[j - 2]
                        g = n["job"] + j - 2
                        act.wait_ge(wT_ready, g + 1)
                        if g >= 2:
                            act.wait_ge(v_ready, HEADS * DEPTH + g - 1)
                        w = 512 if t < 2 else 256
                        nc.scalar.copy(wT[:, (j - 2) % 2, 0:w], bank(6, 0, w)).then_inc(wT_copied, 1)
                n["job"] += len(jobs)
                n["hg"] += 6
                mix_out(s, mixT2)

            def grow_out(s):
                streams, first_bank, _ = rows_wanted(s)
                for st in range(streams):
                    act.wait_ge(g_ready, n["g"] + 1)
                    nc.scalar.copy(grow[:, st, :], ps[:, BANK * (first_bank + 2 * st):BANK * (first_bank + 2 * st + 2)]
                                   ).then_inc(grow_ready, 1)
                    n["g"] += 1

            def square_y(s):
                for t in range(s["tt"]):
                    if t < s["tt"] - 1:
                        act.wait_ge(y_ready, n["y"] + t + 1)
                    else:
                        act.wait_ge(w_used, LEAD + s["u_tall"] + s["k"])
                    nc.scalar.activation(rows[:, t, :], ps[:, 1024 * t:1024 * t + 1024], ACT.Square,
                                         accum_out=sq[:, t:t + 1]).then_inc(sq_done, 1)

            act.wait_ge(consts_landed, 16 * n_consts)
            nc.scalar.activation(cT[:, :, :], cT[:, :, :], ACT.Silu).then_inc(c_silu, 1)
            act.wait_ge(lam_ready, 1)
            nc.scalar.activation(lsum[:, :, :], lsum[:, :, :], ACT.Exp).then_inc(lexp_ready, 1)
            for u in range(3):
                split_hi(SUBS[0], "u_wide", u, 0)
            for i, s in enumerate(SUBS):
                if i == 0:
                    act.wait_ge(x_landed, 16)
                if i == 2 * DEPTH:
                    for t in range(2):
                        act.wait_ge(x_ready, n["x"] - 1 + t)
                        nc.scalar.activation(rows[:, t, :], x[:, t, :], ACT.Square, accum_out=sq[:, t:t + 1]).then_inc(sq_done, 1)
                    n["x"] += 2
                n_tiles = 2 if i == 2 * DEPTH else SUBS[i - 1]["tt"]
                for t in range(s["tw"]):
                    if i and t < n_tiles:
                        act.wait_ge(x_ready, n["x"] - n_tiles + t + 1)
                    nc.scalar.activation(rows[:, t, :], x[:, t, :], ACT.Square, accum_out=sq[:, t:t + 1]).then_inc(sq_done, 1)
                split_hi(s, "u_wide", 3, 0)
                split_rows(s["tw"])
                n["tr"] += 2 * s["tw"]
                wide(s)
                if s["kind"] == "ret":
                    retention_and_stick(s)
                if s["kind"] == "mix":
                    mixer2(s)
                tall(s)
                if i + 1 < len(SUBS):
                    for u in range(3):
                        split_hi(SUBS[i + 1], "u_wide", u, 0)
                if s["blk"] == 2:
                    square_y(s)
                n["y"] += s["tt"] - 1
                n["x"] += s["tt"]

        @block.vector
        def _(dve):
            n = Counter()

            def link(ins):
                n["link"] += 1
                ins.then_inc(dve_link, 1)
                dve.wait_ge(dve_link, n["link"])

            def split_lo(s, key, j, i):
                u = s[key] + j
                slot = u % RING
                dve.wait_ge(hi_done, u + 1 + 4 * i)
                nc.vector.tensor_tensor(wlo[:, slot, :], raw[:, slot, :], whi[:, slot, :].bitcast(F32),
                                        ALU.subtract).then_inc(w_split, 1)

            def mean_square(st):
                n["sq"] += 2
                dve.wait_ge(sq_done, n["sq"])
                nc.vector.tensor_scalar(ms[:, 2 * st:2 * st + 2], sq[:, 2 * st:2 * st + 2], 1.0 / D, EPS,
                                        ALU.mult, ALU.add).then_inc(ms_ready, 1)

            def rstd_wait():
                n["rstd"] += 1
                dve.wait_ge(rstd_ready, n["rstd"])

            def norm_rows(tiles):
                for st in range(tiles // 2):
                    mean_square(st)
                    rstd_wait()
                    for t in (2 * st, 2 * st + 1):
                        nc.vector.tensor_scalar(rows[:, t, :], x[:, t, :], rstd[:, t:t + 1], None, ALU.mult).then_inc(xn_ready, 1)

            def split_rows(s):
                streams = s["tw"] // 2
                items = [(st, k) for k in range(KD) for st in range(streams)]

                def scaled(i):
                    st, k = items[i]
                    if k % 2 == 0:
                        dve.wait_ge(tr_ready, n["tr"] + streams * (k // 2) + st + 1)
                    if s["blk"] == 1:
                        which = c_n1(s["l"]) if s["kind"] == "ret" else c_n2(s["l"])
                        sa, sb_ = cols[:, which, k:k + 1], zero[:, 0:1]
                    else:
                        sa = acol[:, st, k:k + 1]
                        sb_ = modT[:, s["l"], 3 * s["j"] * KD + k, st:st + 1]
                    src = bank(pair_bank(s, k // 2, st), 256 * (k % 2), 256 * (k % 2) + 256)
                    if n["f"] + i >= 4:
                        dve.wait_ge(xs_ready, n["f"] + i - 3)
                    nc.vector.tensor_scalar(fbuf[:, (n["f"] + i) % 4, :], src, sa, sb_, ALU.mult, ALU.add).then_inc(f_ready, 1)

                def rest(i):
                    st, k = items[i]
                    dve.wait_ge(xhi_ready, n["f"] + i + 1)
                    nc.vector.tensor_tensor(xlo[:, k, 256 * st:256 * st + 256], fbuf[:, (n["f"] + i) % 4, :],
                                            xhi[:, k, 256 * st:256 * st + 256].bitcast(F32), ALU.subtract).then_inc(xs_ready, 1)

                scaled(0)
                scaled(1)
                for i in range(len(items)):
                    if i + 2 < len(items):
                        scaled(i + 2)
                    rest(i)
                n["tr"] += 2 * s["tw"]
                n["f"] += len(items)

            def wide(s):
                tw = s["tw"]

                def gates(c, par):
                    for t in range(tw):
                        dve.wait_ge(silu_done, s["gate0"] + t + 1 + tw * c)
                        dve.wait_ge(hT_done, LEAD + s["gate0"] - tw + t + 1 + tw * c)
                        nc.vector.tensor_tensor(hrow[:, t, :], sgate[:, t, :], bank(tw * par + t, 256, 512),
                                                ALU.mult).then_inc(gate_done, 1)

                def mod_out(c):
                    dve.wait_ge(mod_used, LEAD + 4 * s["mod0"] + 4 + 4 * c)
                    at0 = 4 * (s["mod0"] % MOD_CHUNKS)
                    for st in range(2):
                        dst = modT[:, s["l"], :, st][:, bass.ds(4 * c + at0, 4)]
                        src = ps[:, 4 * BANK + st:4 * BANK + 8:2]
                        last = nc.vector.tensor_tensor(dst, src, bmod[:, s["l"], bass.ds(4 * c + at0, 4)], ALU.add)
                    last.then_inc(mod_taken, 1)

                def chunk(c, par, first):
                    if first:
                        return
                    split_lo(s, "u_wide", 0, c)
                    split_lo(s, "u_wide", 1, c)
                    if not first:
                        if s["mod"]:
                            mod_out(c - 1)
                        if s["kind"] == "ffn":
                            gates(c - 1, 1 - par)
                    split_lo(s, "u_wide", 2, c)
                    split_lo(s, "u_wide", 3, c)

                wide_loop(dve, s, chunk)
                if s["kind"] == "ffn":
                    tall_first(s)
                    gates(s["chunks"] - 1, 0)
                if s["mod"]:
                    mod_out(s["chunks"] - 1)

            def tall_unit(s):
                tt = s["tt"]
                src = hid if s["kind"] == "ffn" else (mixT1 if s["kind"] == "ret" else mixT2)
                aring = RING if tt == 2 else 2

                def unit(k, j, i, final):
                    aslot = j % aring
                    w = P * tt
                    dve.wait_ge(hi_done, s["u_tall"] + 1 + k)
                    nc.vector.tensor_tensor(alo[:, w * aslot:w * aslot + w],
                                            src[:, k, 0:w] if isinstance(k, int) else src[:, bass.ds(k, 1), 0:w],
                                            ahi[:, w * aslot:w * aslot + w].bitcast(F32), ALU.subtract)
                    split_lo(s, "u_tall", j, i)

                return unit

            def tall_first(s):
                for k in range(2):
                    tall_unit(s)(k, k, 0, False)

            def tall(s):
                tall_loop(dve, s, tall_unit(s), 2 if s["kind"] == "ffn" else 0)

            def add_y1(s):
                for t in range(2):
                    if t == 0:
                        dve.wait_ge(y_ready, n["y"] + 1)
                    else:
                        dve.wait_ge(w_used, LEAD + s["u_tall"] + s["k"])
                    nc.vector.tensor_tensor(x[:, t, :], x[:, t, :], ps[:, 1024 * t:1024 * t + 1024], ALU.add).then_inc(x_ready, 1)
                n["y"] += 1
                n["x"] += 2

            def add_y2(s):
                tt = s["tt"]
                for st in range(tt // 2):
                    mean_square(st)
                for st in range(tt // 2):
                    rstd_wait()
                    for t in (2 * st, 2 * st + 1):
                        ins = nc.vector.scalar_tensor_tensor(rows[:, t, :], ps[:, 1024 * t:1024 * t + 1024], rstd[:, t:t + 1],
                                                             grow[:, st, :], ALU.mult, ALU.mult)
                        if t % 2 == 0:
                            ins.then_inc(dve_link, 1)
                            n["link"] += 1
                        else:
                            link(ins)
                    for t in (2 * st, 2 * st + 1):
                        nc.vector.tensor_tensor(x[:, t, :], x[:, t, :], rows[:, t, :], ALU.add).then_inc(x_ready, 1)
                n["x"] += tt

            def retention_and_stick(s):
                l = s["l"]
                scale = float(P) ** -0.5

                def head_scores(h):
                    g = 8 * l + h
                    dve.wait_ge(z_ready, g + 1)
                    z = bank(2 + h % 2, 0, 384)
                    if h < 4:
                        if g >= 4:
                            dve.wait_ge(v_ready, g - 3)
                        nc.vector.tensor_tensor(wts[:, h % 4, :], z, rmask[:, h, :], ALU.mult).then_inc(z_taken, 1)
                        return
                    gs = 4 * l + h - 4
                    zz, e, r, lm = (v[:, h % 2, :] for v in (zs, es, rs_, ls))
                    if h >= 6:
                        dve.wait_ge(w_ready, gs - 1)
                    ins = nc.vector.tensor_scalar(zz, z, scale, None, ALU.mult)
                    ins.then_inc(z_scaled, 1)
                    dve.wait_ge(z_scaled, gs + 1)
                    link(nc.vector.tensor_scalar(r, zz, 0.0, None, ALU.max))
                    dve.wait_ge(l_ready, gs + 1)
                    link(nc.vector.tensor_tensor(r, r, e, ALU.add))
                    if h >= 6:
                        dve.wait_ge(s_ready, gs - 1)
                    nc.vector.scalar_tensor_tensor(lm, future[:, :], 1.0, r, ALU.subtract, ALU.mult).then_inc(lm_ready, 1)
                    link(nc.vector.scalar_tensor_tensor(zz, future[:, :], NEG, zz, ALU.mult, ALU.add))

                def head_exponent(h):
                    gs = 4 * l + h - 4
                    dve.wait_ge(s_ready, gs + 1)
                    zz = zs[:, h % 2, :]
                    nc.vector.tensor_tensor(zz, zz, bank(2 + h % 2, 0, 384), ALU.add).then_inc(z_taken, 1)

                def head_stats(h):
                    dve.wait_ge(o_copied, 8 * l + h + 1)
                    for t in range(2):
                        nc.vector.bn_stats(stats[:, 8 * t + h, :], rows[:, t, P * h:P * h + P]).then_inc(dve_link, 1)
                        n["link"] += 1
                for i in range(HEADS + 3):
                    if 0 <= i - 1 < HEADS:
                        head_scores(i - 1)
                    if 4 <= i - 2 < HEADS:
                        head_exponent(i - 2)
                    if 0 <= i - 3 < HEADS:
                        head_stats(i - 3)
                dve.wait_ge(dve_link, n["link"])
                for i in range(16):
                    last = nc.vector.bn_aggr(mv[:, i, :], stats[:, i, :])
                link(last)
                msv = ms[:, 0:16].rearrange("p (t h) -> p t h", t=2)
                mvv = mv[:, :, :].rearrange("p (t h) c -> p t h c", t=2)
                link(nc.vector.tensor_scalar(msv[:, :, 0:4], mvv[:, :, 0:4, 1], EPS, None, ALU.add))
                link(nc.vector.tensor_tensor(msv[:, :, 4:8], mvv[:, :, 4:8, 0], mvv[:, :, 4:8, 0], ALU.mult))
                link(nc.vector.tensor_tensor(msv[:, :, 4:8], msv[:, :, 4:8], mvv[:, :, 4:8, 1], ALU.add))
                nc.vector.tensor_scalar(msv[:, :, 4:8], msv[:, :, 4:8], EPS, None, ALU.add).then_inc(ms_ready, 1)
                n["rstd"] += 1
                dve.wait_ge(rstd_ready, n["rstd"])
                dve.wait_ge(rg_done, 2 * l + 2)
                for t in range(2):
                    for h in range(HEADS):
                        r = rows[:, t, P * h:P * h + P]
                        i = 8 * t + h
                        mean = mv[:, i, 0:1] if h < 4 else zero[:, 0:1]
                        last = nc.vector.tensor_scalar(r, r, mean, rstd[:, i:i + 1], ALU.subtract, ALU.mult)
                    link(last)
                    nc.vector.tensor_tensor(rows[:, t, 0:512], rows[:, t, 0:512], proj1[:, t, RG:RG + 512],
                                            ALU.mult).then_inc(mix_ready, 1)
                mix_out(s, mixT1)

            def mix_out(s, dst):
                if s["kind"] == "mix":
                    dve.wait_ge(grow_ready, n["g"])
                for st in range(s["tt"] // 2):
                    for pair in (0, 2):
                        dve.wait_ge(tr_ready, n["tr"] + 4 * st + pair + 1)
                        for kk in range(2):
                            k = 2 * pair + kk
                            col = cols[:, c_mix1(s["l"]), k:k + 1] if s["kind"] == "ret" else mixcol[:, k:k + 1]
                            last = nc.vector.tensor_scalar(dst[:, k, 256 * st:256 * st + 256],
                                                           bank(4 * st + pair, 256 * kk, 256 * kk + 256), col, None, ALU.mult)
                        last.then_inc(mixT_dve, 1)
                n["tr"] += 2 * s["tt"]
                n["mixT"] += s["tt"]
                dve.wait_ge(mixT_dve, n["mixT"])
                dve.wait_ge(mixT_act, n["mixT"])

            def mixer2(s):
                l, tt = s["l"], s["tt"]
                jobs = jobs_of(s)
                scale = 64 ** -0.5
                dve.wait_ge(ws_landed, 32 * (l + 1))
                for t in range(tt):
                    dve.wait_ge(gelu_done, n["gelu"] + t + 1)
                    link(nc.vector.tensor_tensor(vsq[:, t, :], proj2[:, t, 256:512], proj2[:, t, 256:512], ALU.mult))
                    link(nc.vector.tensor_reduce(ms[:, 4 * t:4 * t + 4], vsq[:, t, :].rearrange("p (h c) -> p h c", h=4),
                                                 AX_X, ALU.add))
                n["gelu"] += tt
                nc.vector.tensor_scalar(ms[:, 0:4 * tt], ms[:, 0:4 * tt], 1.0 / 64, EPS, ALU.mult, ALU.add).then_inc(ms_ready, 1)
                n["rstd"] += 1
                dve.wait_ge(rstd_ready, n["rstd"])
                for t in range(tt):
                    for h in range(4):
                        v = proj2[:, t, 256 + 64 * h:256 + 64 * h + 64]
                        last = nc.vector.scalar_tensor_tensor(v, v, rstd[:, 4 * t + h:4 * t + h + 1],
                                                              vgain[:, l, 64 * h:64 * h + 64], ALU.mult, ALU.mult)
                    last.then_inc(v_scaled, 1)
                for t in range(tt):
                    dve.wait_ge(mixed_ready, n["mixed"] + t + 1)
                    for h in range(4):
                        last = nc.vector.scalar_tensor_tensor(rows[:, t, 64 * h:64 * h + 64], bank(t, 64 * h, 64 * h + 64),
                                                              bcol[:, l, h:h + 1], proj2[:, t, 64 * h:64 * h + 64],
                                                              ALU.add, ALU.mult)
                    last.then_inc(o_copied, 1)
                n["mixed"] += tt

                def maxima(j):
                    kind, hg, m, t = jobs[j]
                    dve.wait_ge(z_ready, HEADS * DEPTH + n["job"] + j + 1)
                    b, w = 2 * (j % 2), 512 if t < 2 else 256
                    if kind == "C" and t < 2:
                        link(nc.vector.tensor_tensor(bank(b, 0, 256), bank(b, 0, 256), wmask[:, t, :], ALU.add))
                    for i in range(2 if kind == "B" else 1):
                        last = nc.vector.reduce_max(mx[:, j % 2, i:i + 1], bank(b + i, 0, w), AX_X)
                    link(last)
                    if kind == "B":
                        nc.vector.tensor_scalar(nb[:, j % 3, :], mx[:, j % 2, :], -scale, None, ALU.mult).then_inc(max_ready, 1)
                    else:
                        head = 2 * m + (hg - 4)
                        nc.vector.tensor_scalar(nb[:, j % 3, 0:1], mx[:, j % 2, 0:1], -scale, nsink[:, l, head:head + 1],
                                                ALU.mult, ALU.min).then_inc(max_ready, 1)

                def weights(j):
                    kind, hg, m, t = jobs[j]
                    dve.wait_ge(exp_ready, n["job"] + j + 1)
                    slot, w = j % 3, 512 if t < 2 else 256
                    p0, p1 = prob[:, slot, 0, 0:w], prob[:, slot, 1, 0:w]
                    if kind == "B":
                        link(nc.vector.reciprocal(rden[:, :], den[:, slot, :]))
                        link(nc.vector.tensor_scalar(rden[:, 1:2], rden[:, 1:2], nlam[:, l:l + 1], None, ALU.mult))
                        link(nc.vector.tensor_scalar(p1, p1, rden[:, 1:2], None, ALU.mult))
                        nc.vector.scalar_tensor_tensor(p0, p0, rden[:, 0:1], p1, ALU.mult, ALU.add).then_inc(prob_ready, 1)
                    else:
                        link(nc.vector.tensor_tensor(den[:, slot, 0:1], den[:, slot, 0:1], esink[:, slot:slot + 1], ALU.add))
                        link(nc.vector.reciprocal(rden[:, 0:1], den[:, slot, 0:1]))
                        nc.vector.tensor_scalar(p0, p0, rden[:, 0:1], None, ALU.mult).then_inc(prob_ready, 1)

                def output(j):
                    kind, hg, m, t = jobs[j]
                    dve.wait_ge(v_ready, HEADS * DEPTH + n["job"] + j + 1)
                    c0, w = (256 + P * hg, P) if kind == "B" else (768 + 64 * (2 * m + hg - 4), 64)
                    nc.vector.tensor_copy(rows[:, t, c0:c0 + w], bank(7, 0, w)).then_inc(o_copied, 1)
                    n["o"] = HEADS * DEPTH

                for j in range(len(jobs) + 3):
                    if j < len(jobs):
                        maxima(j)
                    if 0 <= j - 1 < len(jobs):
                        weights(j - 1)
                    if 0 <= j - 3 < len(jobs):
                        output(j - 3)
                n["job"] += len(jobs)
                n["oa"] += tt
                dve.wait_ge(o_copied, HEADS * DEPTH + n["job"] + n["oa"])
                for t in range(tt):
                    for h in range(4):
                        last = nc.vector.bn_stats(stats[:, 4 * t + h, :], rows[:, t, 256 + P * h:256 + P * h + P])
                link(last)
                for i in range(4 * tt):
                    last = nc.vector.bn_aggr(mv[:, i, :], stats[:, i, :])
                link(last)
                m_ = ms[:, 0:4 * tt]
                link(nc.vector.tensor_tensor(m_, mv[:, 0:4 * tt, 0], mv[:, 0:4 * tt, 0], ALU.mult))
                link(nc.vector.tensor_tensor(m_, m_, mv[:, 0:4 * tt, 1], ALU.add))
                nc.vector.tensor_scalar(m_, m_, EPS, None, ALU.add).then_inc(ms_ready, 1)
                n["rstd"] += 1
                dve.wait_ge(rstd_ready, n["rstd"])
                for t in range(tt):
                    for h in range(4):
                        r = rows[:, t, 256 + P * h:256 + P * h + P]
                        last = nc.vector.tensor_scalar(r, r, rstd[:, 4 * t + h:4 * t + h + 1], None, ALU.mult)
                    last.then_inc(mix_ready, 1)
                mix_out(s, mixT2)

            def sub_columns(s):
                l, j = s["l"], s["j"]
                weight = 1.0 if j == 1 else 0.5
                streams = s["tt"] // 2
                for st in range(s["tw"] // 2):
                    sc = modT[:, l, (3 * j + 1) * KD:(3 * j + 2) * KD, st]
                    last = nc.vector.scalar_tensor_tensor(acol[:, st, :], sc, 1.0, cols[:, c_pre(l, j), :], ALU.add, ALU.mult)
                for st in range(streams):
                    gt = modT[:, l, (3 * j + 2) * KD:(3 * j + 3) * KD, st]
                    last = nc.vector.scalar_tensor_tensor(gcol[:, st, :], gt, weight, post[:, c_post(l, j), :], ALU.mult, ALU.mult)
                if j == 1:
                    nc.vector.memset(mixcol[:, 0:2], 1.0)
                    nc.vector.memset(mixcol[:, 6:8], 1.0)
                    for k in range(2, 6):
                        last = nc.vector.tensor_scalar(mixcol[:, k:k + 1], cols[:, 13 + l, 0:1], 1.0 - LAM_INIT[l], None, ALU.mult)
                last.then_inc(cols_ready, 1)

            dve.sem_inc(gate_done, LEAD)
            dve.sem_inc(mod_taken, 1)
            nc.vector.memset(ones[:, :], 1.0)
            nc.vector.memset(zero[:, :], 0.0)
            link(nc.vector.memset(mhalf[:, :], -0.5))
            dve.wait_ge(consts_landed, 16 * n_consts)
            link(nc.vector.tensor_tensor(lprod[:, :, :, :], lamw[:, :, 0:4:2, :], lamw[:, :, 1:4:2, :], ALU.mult))
            nc.vector.tensor_reduce(lsum[:, :, :], lprod[:, :, :, :], AX_X, ALU.add).then_inc(lam_ready, 1)
            link(nc.vector.tensor_scalar(nsink[:, :, :], sink[:, :, :], -1.0, None, ALU.mult))
            dve.wait_ge(lexp_ready, 1)
            link(nc.vector.tensor_tensor(nlam[:, :], lsum[:, :, 1], lsum[:, :, 0], ALU.subtract))
            for l in range(DEPTH):
                link(nc.vector.tensor_scalar(nlam[:, l:l + 1], nlam[:, l:l + 1], -LAM_INIT[l], None, ALU.add))
            for u in range(3):
                split_lo(SUBS[0], "u_wide", u, 0)
            dve.wait_ge(x_landed, 16)
            for i, s in enumerate(SUBS):
                if i == 2 * DEPTH:
                    mean_square(0)
                    rstd_wait()
                    dve.wait_ge(grow_ready, 1)
                    n["g"] += 1
                    for t in range(2):
                        nc.vector.scalar_tensor_tensor(x[:, t, :], x[:, t, :], rstd[:, t:t + 1], grow[:, 0, :],
                                                       ALU.mult, ALU.mult).then_inc(x_ready, 1)
                    n["x"] += 2
                if i:
                    dve.wait_ge(x_ready, n["x"])
                if s["blk"] == 2:
                    n["g"] += s["tt"] // 2
                    dve.wait_ge(cols_ready, 2 + i - 2 * DEPTH)
                if s["blk"] == 1 and rows_wanted(s)[0]:
                    nc.vector.tensor_copy(gcol[:, 0, :], cols[:, C_FINAL, :]).then_inc(cols_ready, 1)
                norm_rows(s["tw"])
                split_lo(s, "u_wide", 3, 0)
                split_rows(s)
                wide(s)
                if s["kind"] == "ret":
                    retention_and_stick(s)
                if s["kind"] == "mix":
                    mixer2(s)
                if s["kind"] == "ffn":
                    dve.wait_ge(chunk_taken, taken_total(s))
                tall(s)
                if i + 1 < len(SUBS):
                    for u in range(3):
                        split_lo(SUBS[i + 1], "u_wide", u, 0)
                    if SUBS[i + 1]["blk"] == 2:
                        dve.wait_ge(diag_ready, n["g"] + (i == 2 * DEPTH - 1))
                        sub_columns(SUBS[i + 1])
                if s["blk"] == 1:
                    add_y1(s)
                else:
                    dve.wait_ge(grow_ready, n["g"])
                    add_y2(s)

        @block.gpsimd
        def _(pool):
            n = Counter()

            def link(ins):
                n["link"] += 1
                ins.then_inc(pool_link, 1)
                pool.wait_ge(pool_link, n["link"])

            def inverse_root(m, m0=0):
                n["ms"] += 1
                pool.wait_ge(ms_ready, n["ms"])
                nc.gpsimd.tensor_tensor(rstd[:, m0:m], ms[:, m0:m], mhalf[:, m0:m], ALU.pow).then_inc(rstd_ready, 1)

            def inverse_roots(tiles):
                for st in range(tiles // 2):
                    inverse_root(2 * st + 2, 2 * st)

            def diagonals(s):
                streams, _, diag = rows_wanted(s)
                if not streams:
                    return
                n["cols"] += 1
                pool.wait_ge(cols_ready, n["cols"])
                if s["blk"] == 1:
                    pool.wait_ge(w_used, LEAD + s["u_wide"] + 1)
                for st in range(streams):
                    for k in range(KD):
                        last = nc.gpsimd.tensor_scalar(diag[:, st, k, :], ident[:, :], gcol[:, st, k:k + 1], None, ALU.mult)
                    last.then_inc(diag_ready, 1)

            def rope(view, cos, tmp, swap):
                t1, t2 = tmp
                link(nc.gpsimd.tensor_tensor(t1, view, cos, ALU.mult))
                for dst, src, sn in swap:
                    last = nc.gpsimd.tensor_tensor(dst, src, sn, ALU.mult)
                link(last)
                link(nc.gpsimd.tensor_tensor(view, t1, t2, ALU.add))

            def rope_first(s):
                pool.wait_ge(chunk_taken, LEAD + s["take0"] + 4)
                for t in range(2):
                    v = proj1[:, t, 0:D]
                    t1, t2 = rope1[:, 0, :], rope1[:, 1, :]
                    v8, t18, t28 = (q.rearrange("p (h c) -> p h c", h=8) for q in (v, t1, t2))
                    cos = cs1[:, t, 0, :].unsqueeze(1).broadcast_to([P, 8, P])
                    sins = [cs1[:, t, 1, 64 * i:64 * i + 64].unsqueeze(1).broadcast_to([P, 8, 64]) for i in range(2)]
                    swap = [(t28[:, :, 64 * i:64 * i + 64], v8[:, :, 64 - 64 * i:128 - 64 * i], sins[i]) for i in range(2)]
                    rope(v8, cos, (t18, t28), swap)
                    pool.sem_inc(rope_done, 1)

            def rope_second(s):
                for c0, w in ((QB, 512), (QC, 256), (KB, 512), (KC, 128)):
                    pool.wait_ge(chunk_taken, LEAD + s["take0"] + s["tw"] * ((c0 + w - 1) // CH + 1))
                    for t in range(2):
                        g = w // 64
                        v, t1, t2 = proj2[:, t, c0:c0 + w], rope2[:, 0, 0:w], rope2[:, 1, 0:w]
                        v8, t18 = (q.rearrange("p (h c) -> p h c", h=g) for q in (v, t1))
                        cos = cs2[:, t, 0, :].unsqueeze(1).broadcast_to([P, g, 64])
                        swap = []
                        v5, t5 = (q.rearrange("p (h a b c) -> p h a b c", h=g, a=2, b=2) for q in (v, t2))
                        s5 = cs2[:, t, 1, :].rearrange("p (a b c) -> p a b c", a=2, b=2)
                        for b in range(2):
                            swap.append((t5[:, :, :, b, :], v5[:, :, :, 1 - b, :],
                                         s5[:, :, b, :].unsqueeze(1).broadcast_to([P, g, 2, 16])))
                        t28 = t2.rearrange("p (h c) -> p h c", h=g)
                        rope(v8, cos, (t18, t28), swap)
                        pool.sem_inc(rope_done, 1)

            pool.wait_ge(dve_link, 1)
            for i, s in enumerate(SUBS):
                if i == 2 * DEPTH:
                    inverse_root(2)
                inverse_roots(s["tw"])
                diagonals(s)
                if s["kind"] == "ret":
                    rope_first(s)
                    inverse_root(16)
                if s["kind"] == "mix":
                    rope_second(s)
                    pool.wait_ge(w_used, LEAD + s["u_wide"] + 4 * s["chunks"])
                    pool.dma_start(ws[:, :, :], a["ws"][s["l"]]).then_inc(ws_landed, 16)
                    pool.dma_start(wmask[:, :, :], a["wmask"]).then_inc(ws_landed, 16)
                    inverse_root(4 * s["tt"])
                    inverse_root(4 * s["tt"])
                if s["blk"] == 2:
                    inverse_roots(s["tt"])


def shape_constants():
    import numpy as np
    f = np.float32
    c = {"ident": np.eye(P, dtype=f)}
    pos = np.arange(256, dtype=f)
    inv = (1.0 / (f(ROPE_BASE) ** (np.arange(0, P, 2, dtype=f) / f(P)))).astype(f)
    ang = pos[:, None] * inv[None, :]
    cos, sin = np.cos(ang), np.sin(ang)
    cs = np.stack([np.concatenate([cos, cos], 1), np.concatenate([-sin, sin], 1)], 1)
    c["cs1"] = cs.reshape(2, P, 2, P).transpose(1, 0, 2, 3)
    row, col = np.repeat(np.arange(4, dtype=f), GRID_W), np.tile(np.arange(GRID_W, dtype=f), 4)
    inv = (f(ROPE_BASE) ** (-np.arange(16, dtype=f) / f(16))).astype(f)
    ar, ac = row[:, None] * inv, col[:, None] * inv
    cos = np.concatenate([np.cos(ar)] * 2 + [np.cos(ac)] * 2, 1)
    sin = np.concatenate([-np.sin(ar), np.sin(ar), -np.sin(ac), np.sin(ac)], 1)
    c["cs2"] = np.stack([cos, sin], 1).reshape(2, P, 2, 64).transpose(1, 0, 2, 3)
    s_, t_ = np.arange(P)[:, None], np.arange(P)[None, :]
    diag = (s_ < t_).astype(f)
    valid = np.concatenate([diag, np.ones((P, P), f), diag], 1)
    c["future"] = 1.0 - valid
    c["tri"] = (s_ >= t_).astype(f)
    heads = []
    for h in range(4):
        log_g = np.log1p(-np.exp2(-5.0 - h))
        parts = []
        for sk, tq in ((0, 0), (0, 1), (1, 1)):
            s, t = s_ + P * sk, t_ + P * tq
            w = np.exp(log_g * np.abs(t - s)) * ((s // CHUNK) <= (t // CHUNK)) * P ** -0.5
            parts.append(w)
        heads.append(np.concatenate(parts, 1))
    c["rmask"] = np.stack(heads, 1).astype(f)
    q = np.arange(256).reshape(2, P)
    keys = np.arange(256)
    c["wmask"] = np.stack([np.where(np.abs(q[t][:, None] - keys[None, :]) <= WINDOW, 0.0, NEG) for t in range(2)], 1).astype(f)
    return {k: np.ascontiguousarray(v.astype(f)) for k, v in c.items()}


def kernel(**inputs):
    import numpy as np
    import concourse.bacc as bacc
    from concourse.bass_utils import run_bass_kernel_spmd

    v = {k: np.asarray(a) for k, a in inputs.items()}
    order = np.arange(2560)
    order[QC:QC + 256] = QC + np.arange(256).reshape(2, 2, 64).transpose(1, 0, 2).reshape(-1)

    def wide_units(*mats):
        w = CH // len(mats)
        m = [a.reshape(KD, P, -1, w) for a in mats]
        m = np.stack(m, 3)
        m = m.reshape(4, 2, P, -1, CH).transpose(3, 0, 2, 1, 4)
        return m.reshape(-1, P, UNIT)

    def tall_units(a):
        return a.reshape(-1, P, D)

    units = []
    for l in range(DEPTH):
        units += [wide_units(v["w_in"][l]), tall_units(v["w_out"][l]),
                  wide_units(v["w_gate"][l], v["w_up"][l]), tall_units(v["w_down"][l])]
    for l in range(DEPTH):
        g, u, d = v["ffn_w_gate_2"][l], v["ffn_w_up_2"][l], v["ffn_w_down_2"][l]
        units += [wide_units(g[0], u[0]), tall_units(d[0]),
                  wide_units(v["w_in_2"][l][:, order]), tall_units(v["w_out_2"][l]),
                  wide_units(g[1], u[1]), tall_units(d[1])]

    def column(a):
        return a.reshape(-1, P).T

    subln = [np.stack([v["diff_subln_2"][l]] + [v["diff_subln_2"][l]] * (KD - 1), 1) for l in range(DEPTH)]
    cols = ([column(v["norm1_g"][l]) for l in range(DEPTH)] + [column(v["norm2_g"][l]) for l in range(DEPTH)]
            + [column(np.concatenate([v["ret_norm_g"][l], v["sb_norm_g"][l]])) for l in range(DEPTH)]
            + [column(v["final_g"])]
            + [column(v["norm_pre_2"][l, j]) for l in range(DEPTH) for j in range(3)] + subln)
    arrays = dict(
        x=v["x"], ctx=v["ctx_2"],
        w=np.concatenate(units, 0),
        w_mod=np.concatenate([wide_units(v["w_mod_2"][l]) for l in range(DEPTH)], 0),
        cols=np.stack(cols, 1),
        post=np.stack([column(v["norm_post_2"][l, j]) for l in range(DEPTH) for j in range(3)], 1),
        bmod=np.stack([column(v["b_mod_2"][l]) for l in range(DEPTH)], 1),
        cT=np.stack([column(v["c_2"][0]), column(v["c_ctx_2"])], 2),
        bcol=v["gmlp_b_s_2"].transpose(2, 0, 1),
        ws=v["gmlp_w_s_2"].transpose(0, 3, 1, 2),
        vgain=v["gmlp_v_gain_2"].reshape(DEPTH, 256),
        lam=v["diff_lambda_2"], sink=v["swa_sink_2"],
        **shape_constants())
    nc = bacc.Bacc("TRN2", target_bir_lowering=False, num_devices=1)
    feeds, aps = {}, {}
    for name, arr in arrays.items():
        arr = np.ascontiguousarray(arr)
        feeds["in_" + name] = arr
        aps[name] = nc.dram_tensor("in_" + name, arr.shape, mybir.dt.from_np(arr.dtype), kind="ExternalInput").ap()
    out = nc.dram_tensor("out", (1, 256, D), F32, kind="ExternalOutput").ap()
    build(nc, aps, out)
    r = run_bass_kernel_spmd(nc, [feeds], core_ids=[0])
    return r.results[0]["out"]
```

```python
from collections import Counter
from contextlib import ExitStack
import math

import concourse.bass as bass
from concourse import mybir

F32 = mybir.dt.float32
F32R = mybir.dt.float32r
ALU = mybir.AluOpType
ACT = mybir.ActivationFunctionType
AX_X = mybir.AxisListType.X

P = 128
D = 1024
KD = D // P
F = 2816
KF = F // P
DEPTH = 2
EPS = 1e-6
BANK = 512
RING = 4
UNIT = 1024
CH = 512
WIN1_CHUNKS = 7
WIN2_CHUNKS = 5
GU_CHUNKS = F // 256
N_MOD = 9
MOD_CHUNKS = N_MOD * D // CH
HEADS = 8
NEG = -1e30
CHUNK = 64
GRID_W = 64
WINDOW = 128
ROPE_BASE = 10000.0
LAM_INIT = [0.8 - 0.6 * math.exp(-0.3 * l) for l in range(DEPTH)]

RQ, RK, RV, RG, SQ, SK, SV = (512 * i for i in range(7))
UV, QB, QC, KB, VB, KC, VC = 0, 512, 1024, 1280, 1792, 2304, 2432


def chunk_tiles(s, c):
    if s["kind"] == "mix" and c < 2:
        return range(s["tt"])
    return range(s["tw"])


def plan():
    subs = []
    for l in range(DEPTH):
        subs.append(dict(kind="ret", blk=1, l=l, tw=2, tt=2, chunks=WIN1_CHUNKS, k=KD, mod=True, norm=("n1", l)))
        subs.append(dict(kind="ffn", blk=1, l=l, tw=2, tt=2, chunks=GU_CHUNKS, k=KF, mod=True, norm=("n2", l)))
    for l in range(DEPTH):
        last = l == DEPTH - 1
        subs.append(dict(kind="ffn", blk=2, l=l, j=0, tw=4, tt=4, chunks=GU_CHUNKS, k=KF, mod=False))
        subs.append(dict(kind="mix", blk=2, l=l, j=1, tw=4, tt=2 if last else 4, chunks=WIN2_CHUNKS, k=KD, mod=False))
        t = 2 if last else 4
        subs.append(dict(kind="ffn", blk=2, l=l, j=2, tw=t, tt=t, chunks=GU_CHUNKS, k=KF, mod=False))
    unit = take = gate = mod = 0
    for s in subs:
        s["u_wide"] = unit
        unit += 4 * s["chunks"]
        s["u_tall"] = unit
        unit += s["k"]
        s["take0"] = take
        take += sum(len(chunk_tiles(s, c)) for c in range(s["chunks"]))
        s["gate0"] = gate
        gate += s["tw"] * s["chunks"] * (s["kind"] == "ffn")
        s["mod0"] = mod
        mod += s["chunks"] * s["mod"]
    return subs, unit, mod


SUBS, N_UNITS, N_MODCH = plan()
LEAD = 4


STICK_FIRST = (4, 5, 6, 7, 0, 1, 2, 3)
SPLIT_BEFORE = 2


def jobs_of(s):
    out = []
    for hg in range(6):
        for t in range(s["tt"]):
            if hg < 4:
                out.append(("B", hg, 0, t))
            else:
                out += [("C", hg, 0, t), ("C", hg, 1, t)]
    return out


def build(nc, a, out):
    ctx = ExitStack()
    with ctx:
        cursor = [max(nc.sbuf_base + 31, 16512) // 32 * 32]
        places = {}

        def at(name, shape, dt, offset):
            return nc.alloc_sbuf_tensor_at(name, shape, dt, offset=offset)

        def region(name, size):
            places[name] = cursor[0]
            cursor[0] += (size + 31) // 32 * 32
            assert cursor[0] <= nc.sbuf_usable_end, (name, cursor[0])
            return places[name]

        def sb(name, shape, dt=F32):
            return at(name, shape, dt, region(name, 4 * math.prod(shape[1:])))

        raw = sb("raw", [P, RING, UNIT])
        whi = sb("whi", [P, RING, UNIT], F32R)
        wlo = sb("wlo", [P, RING, UNIT], F32R)
        x = sb("x", [P, 4, D])
        ahi = sb("ahi", [P, 1024], F32R)
        alo = sb("alo", [P, 1024], F32R)
        rows = sb("rows", [P, 4, D])

        r_m = region("m", 16384)
        mraw = at("mraw", [P, RING, UNIT], F32, r_m)
        mixT2 = at("mixT2", [P, KD, 512], F32, r_m)
        diag2 = at("diag2", [P, 2, KD, P], F32, r_m)
        diag1 = at("diag1", [P, 1, KD, P], F32, places["rows"] + 12288)
        cstat = at("cstat", [P, KD, P], F32R, places["rows"] + 8192)
        ws = at("ws", [P, 4, P], F32, r_m + 8192)
        wmask = at("wmask", [P, 2, 256], F32, r_m + 10240)

        r_x = region("xs", 32768)
        xhi = at("xhi", [P, KD, 512], F32R, r_x)
        xlo = at("xlo", [P, KD, 512], F32R, r_x + 16384)
        xhi1 = at("xhi1", [P, KD, 256], F32R, r_x)
        xlo1 = at("xlo1", [P, KD, 256], F32R, r_x + 8192)
        mhi = at("mhi", [P, 2, UNIT], F32R, r_x + 16384)
        mlo = at("mlo", [P, 2, UNIT], F32R, r_x + 24576)
        qkT = at("qkT", [P, 2, 512], F32, r_x)
        wts = at("wts", [P, 4, 384], F32, r_x + 4096)
        zs = at("zs", [P, 4, 384], F32, r_x + 10240)
        es = at("es", [P, 4, 384], F32, r_x + 16384)
        qT = at("qT", [P, 2, 512], F32, r_x)
        kT = at("kT", [P, 2, 512], F32, r_x + 4096)
        prob = at("prob", [P, 3, 2, 512], F32, r_x + 8192)
        wT = at("wT", [P, 2, 512], F32, r_x + 20480)

        r_h = region("h", 45056)
        hid = at("hid", [P, KF, 512], F32, r_h)
        proj1 = at("proj1", [P, 2, 3584], F32, r_h)
        rope1 = at("rope1", [P, 2, D], F32, r_h + 28672)
        mixT1 = at("mixT1", [P, KD, 256], F32, r_h + 36864)
        proj2 = at("proj2", [P, 4, 2560], F32, r_h)
        rope2 = at("rope2", [P, 2, 512], F32, r_h + 40960)

        r_g = region("g", 8192)
        sgate = at("sgate", [P, 4, 256], F32, r_g)
        vsq = at("vsq", [P, 4, 256], F32, r_g)
        hrow = at("hrow", [P, 4, 256], F32, r_g + 4096)
        fbuf = at("fbuf", [P, 4, 256], F32, r_g + 4096)

        r_row = region("grow", 8192)
        grow = at("grow", [P, 2, D], F32, r_row)
        rmask = at("rmask", [P, 4, 384], F32, r_row)
        cs1 = at("cs1", [P, 2, 2, P], F32, r_row + 6144)

        ident = sb("ident", [P, P])
        ones = sb("ones", [P, P])
        tri = sb("tri", [P, P])
        future = sb("future", [P, 384])
        cs2 = sb("cs2", [P, 2, 2, 64])
        cols = sb("cols", [P, 15, KD])
        zero = sb("zero", [P, 1])
        bmod = sb("bmod", [P, DEPTH, N_MOD * KD])
        cT = sb("cT", [P, KD, 2])
        mrow = at("mrow", [4, CH], F32, region("mrow", 4 * CH))
        sel = sb("sel", [P, 2])
        modT = sb("modT", [P, DEPTH, N_MOD * KD, 2])
        bcol = sb("bcol", [P, DEPTH, 4])
        acol = sb("acol", [P, 2, KD])
        gcol = sb("gcol", [P, 2, KD])
        mixcol = sb("mixcol", [P, KD])
        vgain = sb("vgain", [P, DEPTH, 256])
        lamw = at("lamw", [P, DEPTH, 4, 64], F32, places["rows"])
        lprod = at("lprod", [P, DEPTH, 2, 64], F32, places["rows"] + 4096)
        lsum = sb("lsum", [P, DEPTH, 2])
        nlam = sb("nlam", [P, DEPTH])
        sink = sb("sink", [P, DEPTH, 4])
        nsink = sb("nsink", [P, DEPTH, 4])
        sq = sb("sq", [P, 4])
        ms = sb("ms", [P, 16])
        rstd = sb("rstd", [P, 16])
        mhalf = sb("mhalf", [P, 16])
        stats = sb("stats", [P, 16, 6])
        mv = sb("mv", [P, 16, 2])
        mx = sb("mx", [P, 2, 2])
        nb = sb("nb", [P, 3, 2])
        den = sb("den", [P, 3, 2])
        esink = sb("esink", [P, 3])
        rden = sb("rden", [P, 2])

        ps = ctx.enter_context(nc.psum_tensor("ps", [P, 8 * BANK], F32))

        def bank(b, lo=0, hi=BANK):
            return ps[:, BANK * b + lo:BANK * b + hi]

        def sem(name):
            return ctx.enter_context(nc.semaphore(name))

        consts_landed = sem("consts_landed")
        late_landed = sem("late_landed")
        x_landed = sem("x_landed")
        raw_landed = [sem(f"raw_landed{i}") for i in range(RING)]
        mraw_landed = [sem(f"mraw_landed{i}") for i in range(RING)]
        ws_landed = sem("ws_landed")
        out_landed = sem("out_landed")
        hi_done = sem("hi_done")
        a_hi_done = sem("a_hi_done")
        a_split = sem("a_split")
        w_split = sem("w_split")
        w_used = sem("w_used")
        mod_hi = sem("mod_hi")
        mod_split = sem("mod_split")
        mod_used = sem("mod_used")
        mod_rows = sem("mod_rows")
        mod_cols = sem("mod_cols")
        mod_taken = sem("mod_taken")
        chunk_taken = sem("chunk_taken")
        silu_done = sem("silu_done")
        gate_done = sem("gate_done")
        hT_done = sem("hT_done")
        c_silu = sem("c_silu")
        c_split = sem("c_split")
        sq_done = sem("sq_done")
        ms_ready = sem("ms_ready")
        rstd_ready = sem("rstd_ready")
        xn_ready = sem("xn_ready")
        tr_ready = sem("tr_ready")
        f_ready = sem("f_ready")
        xhi_ready = sem("xhi_ready")
        xs_ready = sem("xs_ready")
        y_ready = sem("y_ready")
        x_ready = sem("x_ready")
        cols_ready = sem("cols_ready")
        diag_ready = sem("diag_ready")
        g_ready = sem("g_ready")
        grow_ready = sem("grow_ready")
        dve_link = sem("dve_link")
        act_link = sem("act_link")
        pool_link = sem("pool_link")
        lam_ready = sem("lam_ready")
        lexp_ready = sem("lexp_ready")
        rope_done = sem("rope_done")
        rg_done = sem("rg_done")
        qkT_ready = sem("qkT_ready")
        qkT_copied = sem("qkT_copied")
        z_ready = sem("z_ready")
        z_taken = sem("z_taken")
        l_ready = sem("l_ready")
        lm_ready = sem("lm_ready")
        s_ready = sem("s_ready")
        exponent_ready = sem("exponent_ready")
        w_ready = sem("w_ready")
        v_ready = sem("v_ready")
        o_copied = sem("o_copied")
        v_scaled = sem("v_scaled")
        mixed_ready = sem("mixed_ready")
        max_ready = sem("max_ready")
        exp_ready = sem("exp_ready")
        prob_ready = sem("prob_ready")
        wT_ready = sem("wT_ready")
        wT_copied = sem("wT_copied")
        mix_ready = sem("mix_ready")
        mixT_dve = sem("mixT_dve")
        mixT_act = sem("mixT_act")

        n_consts = 6
        n_late = 9
        block = ctx.enter_context(nc.Block())

        def c_n1(l):
            return l

        def c_n2(l):
            return 2 + l

        def c_mix1(l):
            return 4 + l

        C_FINAL = 6

        def c_pre(l, j):
            return 7 + 3 * l + j

        post = sb("post", [P, 6, KD])

        def c_post(l, j):
            return 3 * l + j

        def rows_wanted(s):
            if s["blk"] == 2:
                return s["tt"] // 2, s["tw"] if s["tw"] == 4 else 4, diag2
            if s["kind"] == "ffn" and s["l"] == DEPTH - 1:
                return 1, 2, diag1
            return 0, 0, None

        def pair_bank(s, pair, st):
            return 4 + pair if s["tw"] == 2 else 4 + (2 * pair + st) % 4

        def taken(s, c):
            if s["kind"] == "mix":
                return s["take0"] + sum(len(chunk_tiles(s, q)) for q in range(c))
            return s["tw"] * c + s["take0"]

        def taken_total(s):
            return LEAD + taken(s, s["chunks"])

        @block.sync
        def _(sp):
            def load_main(u, slot, first=False):
                if not first:
                    sp.wait_ge(w_split, u - RING + 1)
                sp.dma_start(raw[:, slot, :], a["w"][u]).then_inc(raw_landed[slot], 16)

            def load_mod(m, slot):
                sp.wait_ge(mod_split, m + 1)
                sp.dma_start(mraw[:, slot, :], a["w_mod"][m]).then_inc(mraw_landed[slot], 16)

            sp.dma_start(x[:, 0:2, :], a["x"].rearrange("b (t p) d -> p (b t) d", p=P)).then_inc(x_landed, 16)
            def constant(name, dst, sem_, broadcast=False):
                src = a[name].partition_broadcast(P) if broadcast else a[name]
                sp.dma_start(dst[tuple([slice(None)] * len(dst.shape))], src).then_inc(sem_, 16)

            for name, dst in (("ident", ident), ("cols", cols), ("cT", cT)):
                constant(name, dst, consts_landed)
            for name, dst in (("lam", lamw), ("sink", sink), ("vgain", vgain)):
                constant(name, dst, consts_landed, True)
            for u in range(4):
                load_main(u, u, first=True)
                load_mod(u, u)
            for name, dst in (("cs1", cs1), ("tri", tri), ("future", future), ("rmask", rmask), ("bmod", bmod),
                              ("cs2", cs2), ("post", post), ("bcol", bcol)):
                constant(name, dst, late_landed)
            sp.dma_start(x[:, 2:4, :], a["ctx"].rearrange("b (t p) d -> p (b t) d", p=P)).then_inc(late_landed, 16)
            for s in SUBS:
                done = 1 if s["u_wide"] == 0 else 0
                with sp.Fori(0, s["chunks"] - done) as i:
                    for u in range(4):
                        unit = s["u_wide"] + 4 * done + u
                        load_main(4 * i + unit, unit % RING)
                        if s["mod"]:
                            load_mod(4 * i + (4 * s["mod0"] + 4 * done + u), u)
                loops = s["k"] // 4
                with sp.Fori(0, loops) as i:
                    for u in range(4):
                        unit = s["u_tall"] + u
                        load_main(4 * i + unit, unit % RING)
                for u in range(4 * loops, s["k"]):
                    unit = s["u_tall"] + u
                    load_main(unit, unit % RING)
            sp.wait_ge(x_ready, sum(s["tt"] for s in SUBS) + 2)
            sp.dma_start(out.rearrange("b (t p) d -> p (b t) d", p=P), x[:, 0:2, :]).then_inc(out_landed, 16)
            sp.wait_ge(out_landed, 16)

        def wide_loop(eng, s, body):
            body(0, 0, True)
            if s["kind"] == "mix":
                for c in range(1, s["chunks"]):
                    body(c, c % 2, False)
                return
            with eng.Fori(0, (s["chunks"] - 1) // 2) as i:
                body(2 * i + 1, 1, False)
                body(2 * i + 2, 0, False)

        def tall_loop(eng, s, body, done=0):
            loops = (s["k"] - 1) // 4
            for k in range(done, 4):
                body(k, k, 0, False)
            if loops > 1:
                with eng.Fori(1, loops) as i:
                    for j in range(4):
                        body(4 * i + j, j, i, False)
            for k in range(4 * loops, s["k"]):
                body(k, k % 4, k // 4, k == s["k"] - 1)

        @block.tensor
        def _(pe):
            n = Counter()
            pe.sem_inc(w_used, LEAD)
            pe.sem_inc(mod_used, LEAD)
            pe.sem_inc(hT_done, LEAD)

            def mm(o, lhsT, rhs, start, stop):
                return nc.tensor.matmul(o, lhsT, rhs, start=start, stop=stop, skip_group_check=True)

            def transpose_pair(s, pair):
                streams = s["tw"] // 2
                for st in range(streams):
                    pe.wait_ge(xn_ready, n["xn"] + 2 * (st + 1))
                    if streams == 2 and pair >= 2:
                        pe.wait_ge(f_ready, n["xs"] + streams * (2 * pair - 3) + st + 1)
                    for kk in range(2):
                        for t in range(2):
                            o = bank(pair_bank(s, pair, st), 256 * kk + 128 * t, 256 * kk + 128 * t + 128)
                            last = nc.tensor.transpose(o, rows[:, 2 * st + t, P * (2 * pair + kk):P * (2 * pair + kk + 1)],
                                                       ident[:, :])
                    last.then_inc(tr_ready, 1)

            def broadcast_rows(s):
                streams, first_bank, diag = rows_wanted(s)
                if not streams:
                    return
                pe.wait_ge(chunk_taken, LEAD + taken(s, s["chunks"] - 1))
                for st in range(streams):
                    pe.wait_ge(diag_ready, n["diag"] + st + 1)
                    for k in range(KD):
                        last = mm(bank(first_bank + 2 * st + k // 4, P * (k % 4), P * (k % 4) + P),
                                  ones[:, :], diag[:, st, k, :], True, True)
                    last.then_inc(g_ready, 1)
                n["diag"] += streams

            def wide(s):
                tw = s["tw"]
                streams = tw // 2
                for pair in range(4 if streams == 1 else 2):
                    transpose_pair(s, pair)

                def gate_transposes(c, par):
                    for t in range(tw):
                        pe.wait_ge(gate_done, LEAD + s["gate0"] + tw * c + (t + 1))
                        for h in range(2):
                            last = nc.tensor.transpose(bank(tw * par + t, P * h, P * h + P),
                                                       hrow[:, t, P * h:P * h + P], ident[:, :])
                        last.then_inc(hT_done, 1)

                def mod_columns(c):
                    pe.wait_ge(mod_rows, 2 + s["mod0"] + 1 + c)
                    pe.wait_ge(mod_taken, 1 + s["mod0"] + c)
                    for nt in range(4):
                        last = mm(bank(6, 2 * nt, 2 * nt + 2), mrow[0:4, P * nt:P * nt + P], sel[0:4, :], True, True)
                    last.then_inc(mod_cols, 1)

                def chunk(c, par, first):
                    for u in range(4):
                        slot = (s["u_wide"] + u) % RING
                        pe.wait_ge(w_split, s["u_wide"] + u + 1 + 4 * c)
                        if first:
                            pe.wait_ge(xs_ready, n["xs"] + streams * (2 * u + 2))
                        if u == 0:
                            if not (first and s["take0"] == 0):
                                pe.wait_ge(chunk_taken, LEAD + (s["take0"] if first else taken(s, c - 1)))
                        for kk in range(2):
                            k = 2 * u + kk
                            hi, lo = (w[:, slot, CH * kk:CH * kk + CH] for w in (whi, wlo))
                            for t in chunk_tiles(s, c) if isinstance(c, int) else range(tw):
                                o = bank(tw * par + t)
                                xh, xl = (v[:, k, P * t:P * t + P] for v in ((xhi1, xlo1) if tw == 2 and s["blk"] == 1 else (xhi, xlo)))
                                mm(o, xh, hi, k == 0, False)
                                mm(o, xh, lo, False, False)
                                last = mm(o, xl, hi, False, k == KD - 1)
                        last.then_inc(w_used, 1)
                        if s["mod"]:
                            pe.wait_ge(mod_split, LEAD + 4 * s["mod0"] + u + 1 + 4 * c)
                            if u == 0:
                                pe.wait_ge(mod_rows, 2 + s["mod0"] - 1 + c)
                            for kk in range(2):
                                for m_ in (mhi, mlo):
                                    last = mm(bank(4 + par), cstat[:, 2 * u + kk, :], m_[:, u % 2, CH * kk:CH * kk + CH],
                                              u == kk == 0 and m_ is mhi, u == 3 and kk == 1 and m_ is mlo)
                            last.then_inc(mod_used, 1)
                            if u == 2 and not first:
                                mod_columns(c - 1)
                        if first and streams == 2 and u < 2:
                            transpose_pair(s, u + 2)
                        if u == 1 and not first and s["kind"] == "ffn":
                            gate_transposes(c - 1, 1 - par)

                wide_loop(pe, s, chunk)
                if s["mod"]:
                    mod_columns(s["chunks"] - 1)
                n["xs"] += KD * streams
                n["xn"] += tw
                broadcast_rows(s)
                if s["kind"] == "ffn":
                    gate_transposes(s["chunks"] - 1, 0)

            def tall(s):
                tt = s["tt"]
                pe.wait_ge(chunk_taken, taken_total(s))

                def unit(k, j, i, final):
                    slot = (s["u_tall"] + j) % RING
                    pe.wait_ge(w_split, s["u_tall"] + 1 + k)
                    if s["kind"] != "ffn" and isinstance(k, int) and k < SPLIT_BEFORE:
                        n["as"] += 1
                        pe.wait_ge(a_split, n["as"])
                    aslot = j % (RING if tt == 2 else 2)
                    for t in range(tt):
                        ah, al = (v[:, P * tt * aslot + P * t:P * tt * aslot + P * t + P] for v in (ahi, alo))
                        for h in range(2):
                            hi, lo = (w[:, slot, CH * h:CH * h + CH] for w in (whi, wlo))
                            o = bank(2 * t + h)
                            mm(o, ah, hi, isinstance(k, int) and k == 0, False)
                            mm(o, ah, lo, False, False)
                            last = mm(o, al, hi, False, final)
                        if final and t < tt - 1:
                            last.then_inc(y_ready, 1)
                    last.then_inc(w_used, 1)

                tall_loop(pe, s, unit)

            def retention_and_stick(s):
                l = s["l"]
                pe.wait_ge(chunk_taken, taken_total(s))
                pe.wait_ge(late_landed, 16 * n_late)

                def transposes(p):
                    h, g = STICK_FIRST[p], 8 * l + p
                    if p == 4:
                        pe.wait_ge(rope_done, 2 * (l + 1))
                    if p >= 2:
                        pe.wait_ge(qkT_copied, g - 1)
                    q0, k0 = (RQ + P * h, RK + P * h) if h < 4 else (SQ + P * (h - 4), SK + P * (h - 4))
                    for i, c0 in enumerate((q0, k0)):
                        for t in range(2):
                            last = nc.tensor.transpose(bank(p % 2, 256 * i + P * t, 256 * i + P * t + P),
                                                       proj1[:, t, c0:c0 + P], ident[:, :])
                    last.then_inc(qkT_ready, 1)

                def scores(p):
                    g = 8 * l + p
                    pe.wait_ge(qkT_copied, g + 1)
                    if p >= 2:
                        pe.wait_ge(z_taken, g - 1)
                    b, s_ = 2 + p % 2, p % 2
                    mm(bank(b, 0, 256), qkT[:, s_, 256:384], qkT[:, s_, 0:256], True, True)
                    mm(bank(b, 256, 384), qkT[:, s_, 384:512], qkT[:, s_, 128:256], True, True).then_inc(z_ready, 1)

                def suffix_sums(p):
                    pe.wait_ge(lm_ready, 4 * l + p + 1)
                    if p >= 2:
                        pe.wait_ge(exponent_ready, 4 * l + p - 1)
                    b = 6 + p % 2
                    mm(bank(b, 0, 256), tri[:, :], es[:, p, 0:256], True, False)
                    mm(bank(b, 128, 256), ones[:, :], es[:, p, 256:384], False, True)
                    mm(bank(b, 256, 384), tri[:, :], es[:, p, 256:384], True, True).then_inc(s_ready, 1)

                def values(h):
                    g = 8 * l + h
                    if h < 4:
                        pe.wait_ge(z_taken, g + 4 + 1)
                    else:
                        pe.wait_ge(w_ready, 4 * l + h - 4 + 1)
                    if h >= 2:
                        pe.wait_ge(o_copied, g - 1)
                    c0 = RV + P * h if h < 4 else SV + P * (h - 4)
                    w, b = wts[:, h % 4, :], 4 + h % 2
                    mm(bank(b, 0, P), w[:, 0:P], proj1[:, 0, c0:c0 + P], True, True)
                    mm(bank(b, P, 2 * P), w[:, P:2 * P], proj1[:, 0, c0:c0 + P], True, False)
                    mm(bank(b, P, 2 * P), w[:, 2 * P:3 * P], proj1[:, 1, c0:c0 + P], False, True).then_inc(v_ready, 1)

                for i in range(HEADS + 1):
                    if i < HEADS:
                        transposes(i)
                    if i >= 1:
                        scores(i - 1)
                values(0)
                values(1)
                suffix_sums(0)
                suffix_sums(1)
                values(2)
                values(3)
                suffix_sums(2)
                suffix_sums(3)
                for h in range(4, 8):
                    values(h)
                mix_transposes(s)

            def mix_transposes(s):
                for st in range(s["tt"] // 2):
                    pe.wait_ge(mix_ready, n["mix"] + 2 * (st + 1))
                    for pair in range(4):
                        for kk in range(2):
                            for t in range(2):
                                o = bank(4 * st + pair, 256 * kk + 128 * t, 256 * kk + 128 * t + 128)
                                last = nc.tensor.transpose(o, rows[:, 2 * st + t, P * (2 * pair + kk):P * (2 * pair + kk + 1)],
                                                           ident[:, :])
                        last.then_inc(tr_ready, 1)
                n["mix"] += s["tt"]
                pe.wait_ge(mixT_dve, n["mixT"] + s["tt"])
                pe.wait_ge(mixT_act, n["mixT"] + s["tt"])
                n["mixT"] += s["tt"]

            def mixer2(s):
                l = s["l"]
                jobs = jobs_of(s)
                pe.wait_ge(chunk_taken, taken_total(s))
                pe.wait_ge(ws_landed, 32 * (l + 1))
                for t in range(s["tt"]):
                    pe.wait_ge(v_scaled, n["vs"] + t + 1)
                    for h in range(4):
                        last = mm(bank(t, 64 * h, 64 * h + 64), ws[:, h, :],
                                  proj2[:, t, 256 + 64 * h:256 + 64 * h + 64], True, True)
                    last.then_inc(mixed_ready, 1)
                n["vs"] += s["tt"]
                pe.wait_ge(rope_done, 2 * DEPTH + 8 * (l + 1))

                def transposes(hg):
                    hgg = n["hg"] + hg
                    q0 = QB + P * hg if hg < 4 else QC + P * (hg - 4)
                    k0 = KB + P * hg if hg < 4 else KC
                    if hgg >= 1:
                        pe.wait_ge(qkT_copied, HEADS * DEPTH + hgg)
                    for b, c0, tiles in ((4, q0, s["tt"]), (5, k0, 4)):
                        for t in range(tiles):
                            last = nc.tensor.transpose(bank(b, P * t, P * t + P), proj2[:, t, c0:c0 + P], ident[:, :])
                    last.then_inc(qkT_ready, 1)

                def scores(j):
                    kind, hg, m, t = jobs[j]
                    g = n["job"] + j
                    pe.wait_ge(qkT_copied, HEADS * DEPTH + n["hg"] + hg + 1)
                    if j >= 2:
                        pe.wait_ge(exp_ready, g - 1)
                    elif j == 0:
                        pe.wait_ge(o_copied, HEADS * DEPTH + n["job"] + n["oa"] + s["tt"])
                    keys = (0, 512) if t < 2 else (256, 512)
                    for i, mm_ in enumerate((0, 1) if kind == "B" else (m,)):
                        part = slice(64 * mm_, 64 * mm_ + 64)
                        last = mm(bank(2 * (j % 2) + i, 0, keys[1] - keys[0]), qT[part, hg % 2, P * t:P * t + P],
                                  kT[part, hg % 2, keys[0]:keys[1]], True, True)
                    last.then_inc(z_ready, 1)

                def prob_transposes(j):
                    kind, hg, m, t = jobs[j]
                    g = n["job"] + j
                    pe.wait_ge(prob_ready, g + 1)
                    if g >= 1:
                        pe.wait_ge(wT_copied, g)
                    for i in range(4 if t < 2 else 2):
                        last = nc.tensor.transpose(bank(6, P * i, P * i + P), prob[:, j % 3, 0, P * i:P * i + P], ident[:, :])
                    last.then_inc(wT_ready, 1)

                def values(j):
                    kind, hg, m, t = jobs[j]
                    g = n["job"] + j
                    pe.wait_ge(wT_copied, g + 1)
                    pe.wait_ge(o_copied, HEADS * DEPTH + g + n["oa"] + s["tt"])
                    c0, width = (VB + P * hg, P) if kind == "B" else (VC + 64 * m, 64)
                    tiles = (0, 1, 2, 3) if t < 2 else (2, 3)
                    for i, kt in enumerate(tiles):
                        last = mm(bank(7, 0, width), wT[:, j % 2, P * i:P * i + P], proj2[:, kt, c0:c0 + width],
                                  i == 0, i == len(tiles) - 1)
                    last.then_inc(v_ready, 1)

                transposes(0)
                for j in range(len(jobs) + 3):
                    if j < len(jobs):
                        hg = jobs[j][1]
                        if (j == 0 or jobs[j - 1][1] != hg) and hg < 5:
                            transposes(hg + 1)
                        scores(j)
                    if 0 <= j - 2 < len(jobs):
                        prob_transposes(j - 2)
                    if 0 <= j - 3 < len(jobs):
                        values(j - 3)
                n["job"] += len(jobs)
                n["oa"] += s["tt"]
                n["hg"] += 6
                mix_transposes(s)

            pe.wait_ge(consts_landed, 16 * n_consts)
            pe.wait_ge(c_split, 1)
            for i, s in enumerate(SUBS):
                if i:
                    if i == 2 * DEPTH:
                        n["x"] += 2
                    pe.wait_ge(x_ready, n["x"])
                wide(s)
                if s["kind"] == "ret":
                    retention_and_stick(s)
                if s["kind"] == "mix":
                    mixer2(s)
                tall(s)
                n["x"] += s["tt"]

        @block.scalar
        def _(act):
            n = Counter()
            act.sem_inc(chunk_taken, LEAD)

            def link(ins):
                n["link"] += 1
                ins.then_inc(act_link, 1)
                act.wait_ge(act_link, n["link"])

            def split_hi(s, key, j, i):
                u = s[key] + j
                slot = u % RING
                act.wait_ge(w_used, u + 1 + 4 * i)
                act.wait_ge(raw_landed[slot], 16 * (u // RING + 1) + 16 * i)
                nc.scalar.copy(whi[:, slot, :], raw[:, slot, :]).then_inc(hi_done, 1)

            def split_rows(s):
                tiles, blk = s["tw"], s["blk"]
                for k in range(KD):
                    if k == KD // 2:
                        split_hi(s, "u_wide", 3, 0)
                    for st in range(tiles // 2):
                        act.wait_ge(f_ready, n["f"] + 1)
                        nc.scalar.copy((xhi1 if blk == 1 else xhi)[:, k, 256 * st:256 * st + 256], fbuf[:, n["f"] % 4, :]).then_inc(xhi_ready, 1)
                        n["f"] += 1

            def wide(s):
                tw = s["tw"]

                def silus(c, par):
                    for t in range(tw):
                        if t == 0:
                            act.wait_ge(w_used, LEAD + s["u_wide"] + 4 + 4 * c)
                        act.wait_ge(gate_done, LEAD + s["gate0"] - tw + t + 1 + tw * c)
                        nc.scalar.activation(sgate[:, t, :], bank(tw * par + t, 0, 256), ACT.Silu).then_inc(silu_done, 1)

                def hidden_out(c, par):
                    for t in range(tw):
                        act.wait_ge(hT_done, LEAD + s["gate0"] + t + 1 + tw * c)
                        src = bank(tw * par + t, 0, 256).rearrange("p (k c) -> p k c", k=2)
                        nc.scalar.copy(hid[:, bass.ds(2 * c, 2), P * t:P * t + P], src).then_inc(chunk_taken, 1)

                def proj_out(c, par):
                    dst = proj1 if s["kind"] == "ret" else proj2
                    for t in chunk_tiles(s, c) if isinstance(c, int) else range(tw):
                        if t == 0:
                            act.wait_ge(w_used, LEAD + s["u_wide"] + 4 + 4 * c)
                        if s["kind"] == "mix" and c == 0:
                            if t < s["tt"]:
                                nc.scalar.activation(dst[:, t, 0:CH], bank(tw * par + t), ACT.Gelu_apprx_tanh).then_inc(chunk_taken, 1)
                            continue
                        nc.scalar.copy(dst[:, t, bass.ds(CH * c, CH)], bank(tw * par + t)).then_inc(chunk_taken, 1)

                def mod_hi_part(u, c):
                    act.wait_ge(mod_used, LEAD - 2 + 4 * s["mod0"] + u + 1 + 4 * c)
                    act.wait_ge(mraw_landed[u], 16 * (s["mod0"] + 1) + 16 * c)
                    nc.scalar.copy(mhi[:, u % 2, :], mraw[:, u, :]).then_inc(mod_hi, 1)

                def chunk(c, par, first):
                    ffn, mod = s["kind"] == "ffn", s["mod"]
                    for u in range(4):
                        if not first:
                            split_hi(s, "u_wide", u, c)
                        if u == 1 and not first:
                            if ffn:
                                silus(c - 1, 1 - par)
                            else:
                                proj_out(c - 1, 1 - par)
                        if mod:
                            mod_hi_part(u, c)
                    if not first and ffn:
                        hidden_out(c - 1, 1 - par)

                wide_loop(act, s, chunk)
                c = s["chunks"] - 1
                if s["kind"] == "ffn":
                    tall_first(s)
                    silus(c, 0)
                    grow_out(s)
                    hidden_out(c, 0)
                else:
                    grow_out(s)
                    proj_out(c, 0)

            def tall_unit(s):
                tt = s["tt"]
                src = hid if s["kind"] == "ffn" else (mixT1 if s["kind"] == "ret" else mixT2)
                aring = RING if tt == 2 else 2

                def unit(k, j, i, final):
                    aslot = j % aring
                    act.wait_ge(w_used, LEAD + s["u_tall"] - aring + 1 + k)
                    w = P * tt
                    ins = nc.scalar.copy(ahi[:, w * aslot:w * aslot + w], src[:, k, 0:w] if isinstance(k, int)
                                         else src[:, bass.ds(k, 1), 0:w])
                    if s["kind"] != "ffn" and isinstance(k, int) and k < SPLIT_BEFORE:
                        ins.then_inc(a_hi_done, 1)
                    else:
                        split_hi(s, "u_tall", j, i)

                return unit

            def tall_first(s):
                act.wait_ge(chunk_taken, LEAD + taken(s, s["chunks"] - 1))
                for k in range(2):
                    tall_unit(s)(k, k, 0, False)

            def tall(s):
                if s["kind"] != "ffn":
                    act.wait_ge(mixT_dve, n["mixT"])
                    act.wait_ge(mixT_act, n["mixT"])
                else:
                    act.wait_ge(chunk_taken, taken_total(s))
                tall_loop(act, s, tall_unit(s), 2 if s["kind"] == "ffn" else 0)

            def retention_and_stick(s):
                l = s["l"]

                def silu_gate(t):
                    nc.scalar.activation(proj1[:, t, RG:RG + 512], proj1[:, t, RG:RG + 512], ACT.Silu).then_inc(rg_done, 1)

                def qk_copy(p):
                    g = 8 * l + p
                    act.wait_ge(qkT_ready, g + 1)
                    if p >= 2:
                        act.wait_ge(z_ready, g - 1)
                    nc.scalar.copy(qkT[:, p % 2, :], bank(p % 2)).then_inc(qkT_copied, 1)

                def exp_abs(p):
                    act.wait_ge(z_taken, 8 * l + p + 1)
                    link(nc.scalar.activation(es[:, p, :], zs[:, p, :], ACT.Abs))
                    nc.scalar.activation(es[:, p, :], es[:, p, :], ACT.Exp, scale=-1.0).then_inc(act_link, 1)
                    n["link"] += 1

                def log_all():
                    act.wait_ge(act_link, n["link"])
                    for p in range(4):
                        nc.scalar.activation(es[:, p, :], es[:, p, :], ACT.Ln, bias=1.0).then_inc(l_ready, 1)

                def stick_weights(p):
                    act.wait_ge(exponent_ready, 4 * l + p + 1)
                    act.wait_ge(v_ready, 8 * l + p + 1)
                    nc.scalar.activation(wts[:, p, :], zs[:, p, :], ACT.Exp).then_inc(w_ready, 1)

                def output(h):
                    act.wait_ge(v_ready, 8 * l + h + 1)
                    nc.scalar.copy(rows[:, 0:2, P * h:P * h + P],
                                   bank(4 + h % 2, 0, 256).rearrange("p (t c) -> p t c", t=2)).then_inc(o_copied, 1)

                qk_copy(0)
                qk_copy(1)
                silu_gate(0)
                silu_gate(1)
                for p in range(4):
                    exp_abs(p)
                    qk_copy(p + 2)
                log_all()
                qk_copy(6)
                qk_copy(7)
                output(0)
                output(1)
                stick_weights(0)
                stick_weights(1)
                output(2)
                output(3)
                stick_weights(2)
                stick_weights(3)
                for h in range(4, 8):
                    output(h)
                split_output_weights(s)
                mix_out(s, mixT1)

            def split_output_weights(s):
                for j in range(SPLIT_BEFORE):
                    split_hi(s, "u_tall", j, 0)

            def mix_out(s, dst):
                for st in range(s["tt"] // 2):
                    for pair in (1, 3):
                        act.wait_ge(tr_ready, n["tr"] + 4 * st + pair + 1)
                        for kk in range(2):
                            k = 2 * pair + kk
                            col = cols[:, c_mix1(s["l"]), k:k + 1] if s["kind"] == "ret" else mixcol[:, k:k + 1]
                            last = nc.scalar.activation(dst[:, k, 256 * st:256 * st + 256],
                                                        bank(4 * st + pair, 256 * kk, 256 * kk + 256), ACT.Copy, scale=col)
                        last.then_inc(mixT_act, 1)
                    pass
                n["tr"] += 2 * s["tt"]
                n["mixT"] += s["tt"]

            def mixer2(s):
                l = s["l"]
                jobs = jobs_of(s)
                scale = 64 ** -0.5
                def qk_copy(hg):
                    hgg = n["hg"] + hg
                    act.wait_ge(qkT_ready, HEADS * DEPTH + hgg + 1)
                    nc.scalar.copy(qT[:, hg % 2, 0:P * s["tt"]], bank(4, 0, P * s["tt"]))
                    nc.scalar.copy(kT[:, hg % 2, :], bank(5)).then_inc(qkT_copied, 1)

                qk_copy(0)
                for j in range(len(jobs) + 3):
                    if j < len(jobs):
                        kind, hg, m, t = jobs[j]
                        g = n["job"] + j
                        if (j == 0 or jobs[j - 1][1] != hg) and hg < 5:
                            qk_copy(hg + 1)
                        act.wait_ge(max_ready, g + 1)
                        if g >= 3:
                            act.wait_ge(wT_ready, g - 2)
                        w = 512 if t < 2 else 256
                        b, slot = 2 * (j % 2), j % 3
                        for i in range(2 if kind == "B" else 1):
                            last = nc.scalar.activation(prob[:, slot, i, 0:w], bank(b + i, 0, w), ACT.Exp,
                                                        bias=nb[:, slot, i:i + 1], scale=scale, accum_out=den[:, slot, i:i + 1])
                        if kind == "C":
                            head = 2 * m + (hg - 4)
                            last = nc.scalar.activation(esink[:, slot:slot + 1], sink[:, l, head:head + 1], ACT.Exp,
                                                        bias=nb[:, slot, 0:1])
                        last.then_inc(exp_ready, 1)
                    if 0 <= j - 2 < len(jobs):
                        kind, hg, m, t = jobs[j - 2]
                        g = n["job"] + j - 2
                        act.wait_ge(wT_ready, g + 1)
                        if g >= 2:
                            act.wait_ge(v_ready, HEADS * DEPTH + g - 1)
                        w = 512 if t < 2 else 256
                        nc.scalar.copy(wT[:, (j - 2) % 2, 0:w], bank(6, 0, w)).then_inc(wT_copied, 1)
                n["job"] += len(jobs)
                n["hg"] += 6
                split_output_weights(s)
                mix_out(s, mixT2)

            def grow_out(s):
                streams, first_bank, _ = rows_wanted(s)
                for st in range(streams):
                    act.wait_ge(g_ready, n["g"] + 1)
                    nc.scalar.copy(grow[:, st, :], ps[:, BANK * (first_bank + 2 * st):BANK * (first_bank + 2 * st + 2)]
                                   ).then_inc(grow_ready, 1)
                    n["g"] += 1

            def square_y(s):
                for t in range(s["tt"]):
                    if t < s["tt"] - 1:
                        act.wait_ge(y_ready, n["y"] + t + 1)
                    else:
                        act.wait_ge(w_used, LEAD + s["u_tall"] + s["k"])
                    nc.scalar.activation(rows[:, t, :], ps[:, 1024 * t:1024 * t + 1024], ACT.Square,
                                         accum_out=sq[:, t:t + 1]).then_inc(sq_done, 1)

            act.wait_ge(consts_landed, 16 * n_consts)
            nc.scalar.activation(cT[:, :, :], cT[:, :, :], ACT.Silu).then_inc(c_silu, 1)
            act.wait_ge(lam_ready, 1)
            nc.scalar.activation(lsum[:, :, :], lsum[:, :, :], ACT.Exp).then_inc(lexp_ready, 1)
            for i, s in enumerate(SUBS):
                if i == 0:
                    act.wait_ge(x_landed, 16)
                if i == 2 * DEPTH:
                    act.wait_ge(late_landed, 16 * n_late)
                    for t in range(2):
                        act.wait_ge(x_ready, n["x"] - 1 + t)
                        nc.scalar.activation(rows[:, t, :], x[:, t, :], ACT.Square, accum_out=sq[:, t:t + 1]).then_inc(sq_done, 1)
                    n["x"] += 2
                n_tiles = 2 if i == 2 * DEPTH else SUBS[i - 1]["tt"]
                for t in range(s["tw"]):
                    if i and t < n_tiles:
                        act.wait_ge(x_ready, n["x"] - n_tiles + t + 1)
                    nc.scalar.activation(rows[:, t, :], x[:, t, :], ACT.Square, accum_out=sq[:, t:t + 1]).then_inc(sq_done, 1)
                for u in range(3 if i == 0 else 0):
                    split_hi(s, "u_wide", u, 0)
                split_rows(s)
                n["tr"] += 2 * s["tw"]
                wide(s)
                if s["kind"] == "ret":
                    retention_and_stick(s)
                if s["kind"] == "mix":
                    mixer2(s)
                tall(s)
                if i + 1 < len(SUBS):
                    for u in range(3):
                        split_hi(SUBS[i + 1], "u_wide", u, 0)
                if s["blk"] == 2:
                    square_y(s)
                n["y"] += s["tt"] - 1
                n["x"] += s["tt"]

        @block.vector
        def _(dve):
            n = Counter()

            def link(ins):
                n["link"] += 1
                ins.then_inc(dve_link, 1)
                dve.wait_ge(dve_link, n["link"])

            def split_lo(s, key, j, i):
                u = s[key] + j
                slot = u % RING
                dve.wait_ge(hi_done, u + 1 + 4 * i)
                nc.vector.tensor_tensor(wlo[:, slot, :], raw[:, slot, :], whi[:, slot, :].bitcast(F32),
                                        ALU.subtract).then_inc(w_split, 1)

            def mean_square(st):
                n["sq"] += 2
                dve.wait_ge(sq_done, n["sq"])
                nc.vector.tensor_scalar(ms[:, 2 * st:2 * st + 2], sq[:, 2 * st:2 * st + 2], 1.0 / D, EPS,
                                        ALU.mult, ALU.add).then_inc(ms_ready, 1)

            def rstd_wait():
                n["rstd"] += 1
                dve.wait_ge(rstd_ready, n["rstd"])

            def norm_rows(tiles):
                for st in range(tiles // 2):
                    mean_square(st)
                    rstd_wait()
                    for t in (2 * st, 2 * st + 1):
                        nc.vector.tensor_scalar(rows[:, t, :], x[:, t, :], rstd[:, t:t + 1], None, ALU.mult).then_inc(xn_ready, 1)

            def split_rows(s):
                streams = s["tw"] // 2
                items = [(st, k) for k in range(KD) for st in range(streams)]

                def scaled(i):
                    st, k = items[i]
                    if k % 2 == 0:
                        dve.wait_ge(tr_ready, n["tr"] + streams * (k // 2) + st + 1)
                    if s["blk"] == 1:
                        which = c_n1(s["l"]) if s["kind"] == "ret" else c_n2(s["l"])
                        sa, sb_ = cols[:, which, k:k + 1], zero[:, 0:1]
                    else:
                        sa = acol[:, st, k:k + 1]
                        sb_ = modT[:, s["l"], 3 * s["j"] * KD + k, st:st + 1]
                    src = bank(pair_bank(s, k // 2, st), 256 * (k % 2), 256 * (k % 2) + 256)
                    if n["f"] + i >= 4:
                        dve.wait_ge(xs_ready, n["f"] + i - 3)
                    nc.vector.tensor_scalar(fbuf[:, (n["f"] + i) % 4, :], src, sa, sb_, ALU.mult, ALU.add).then_inc(f_ready, 1)

                def rest(i):
                    st, k = items[i]
                    dve.wait_ge(xhi_ready, n["f"] + i + 1)
                    hi, lo = (xhi1, xlo1) if s["blk"] == 1 else (xhi, xlo)
                    nc.vector.tensor_tensor(lo[:, k, 256 * st:256 * st + 256], fbuf[:, (n["f"] + i) % 4, :],
                                            hi[:, k, 256 * st:256 * st + 256].bitcast(F32), ALU.subtract).then_inc(xs_ready, 1)

                scaled(0)
                scaled(1)
                for i in range(len(items)):
                    if i + 2 < len(items):
                        scaled(i + 2)
                    rest(i)
                    if i == len(items) // 2:
                        split_lo(s, "u_wide", 3, 0)
                n["tr"] += 2 * s["tw"]
                n["f"] += len(items)

            def wide(s):
                tw = s["tw"]

                def gates(c, par):
                    for t in range(tw):
                        dve.wait_ge(silu_done, s["gate0"] + t + 1 + tw * c)
                        dve.wait_ge(hT_done, LEAD + s["gate0"] - tw + t + 1 + tw * c)
                        nc.vector.tensor_tensor(hrow[:, t, :], sgate[:, t, :], bank(tw * par + t, 256, 512),
                                                ALU.mult).then_inc(gate_done, 1)

                def mod_lo_part(u, c):
                    dve.wait_ge(mod_hi, 4 * s["mod0"] + u + 1 + 4 * c)
                    nc.vector.tensor_tensor(mlo[:, u % 2, :], mraw[:, u, :], mhi[:, u % 2, :].bitcast(F32),
                                            ALU.subtract).then_inc(mod_split, 1)

                def mod_rows_out(c, par):
                    dve.wait_ge(mod_used, LEAD + 4 * s["mod0"] + 4 + 4 * c)
                    dve.wait_ge(mod_cols, s["mod0"] + c) if not (isinstance(c, int) and c + s["mod0"] == 0) else None
                    nc.vector.tensor_copy(mrow[0:4, :], ps[0:4, BANK * (4 + par):BANK * (5 + par)]).then_inc(mod_rows, 1)

                def mod_out(c):
                    dve.wait_ge(mod_cols, s["mod0"] + 1 + c)
                    at0 = 4 * (s["mod0"] % MOD_CHUNKS)
                    for st in range(2):
                        dst = modT[:, s["l"], :, st][:, bass.ds(4 * c + at0, 4)]
                        src = ps[:, 6 * BANK + st:6 * BANK + 8:2]
                        last = nc.vector.tensor_tensor(dst, src, bmod[:, s["l"], bass.ds(4 * c + at0, 4)], ALU.add)
                    last.then_inc(mod_taken, 1)

                def chunk(c, par, first):
                    ffn, mod = s["kind"] == "ffn", s["mod"]
                    for u in range(4):
                        if not first:
                            split_lo(s, "u_wide", u, c)
                        if u == 1 and not first:
                            if mod:
                                mod_rows_out(c - 1, 1 - par)
                            if ffn:
                                gates(c - 1, 1 - par)
                        if mod:
                            mod_lo_part(u, c)
                    if not first and mod:
                        mod_out(c - 1)
                    if s["kind"] == "mix" and c == 2:
                        gmlp_norm(s)
                    if s["kind"] == "mix" and c == 4:
                        gmlp_scale(s)

                wide_loop(dve, s, chunk)
                if s["kind"] == "ffn":
                    tall_first(s)
                    gates(s["chunks"] - 1, 0)
                if s["mod"]:
                    mod_rows_out(s["chunks"] - 1, 0)
                    mod_out(s["chunks"] - 1)

            def tall_unit(s):
                tt = s["tt"]
                src = hid if s["kind"] == "ffn" else (mixT1 if s["kind"] == "ret" else mixT2)
                aring = RING if tt == 2 else 2

                def unit(k, j, i, final):
                    aslot = j % aring
                    w = P * tt
                    before = s["kind"] != "ffn" and isinstance(k, int) and k < SPLIT_BEFORE
                    if before:
                        n["ah"] += 1
                        dve.wait_ge(a_hi_done, n["ah"])
                    else:
                        dve.wait_ge(hi_done, s["u_tall"] + 1 + k)
                    ins = nc.vector.tensor_tensor(alo[:, w * aslot:w * aslot + w],
                                                  src[:, k, 0:w] if isinstance(k, int) else src[:, bass.ds(k, 1), 0:w],
                                                  ahi[:, w * aslot:w * aslot + w].bitcast(F32), ALU.subtract)
                    if before:
                        ins.then_inc(a_split, 1)
                    else:
                        split_lo(s, "u_tall", j, i)

                return unit

            def tall_first(s):
                for k in range(2):
                    tall_unit(s)(k, k, 0, False)

            def tall(s):
                tall_loop(dve, s, tall_unit(s), 2 if s["kind"] == "ffn" else 0)

            def add_y1(s):
                for t in range(2):
                    if t == 0:
                        dve.wait_ge(y_ready, n["y"] + 1)
                    else:
                        dve.wait_ge(w_used, LEAD + s["u_tall"] + s["k"])
                    nc.vector.tensor_tensor(x[:, t, :], x[:, t, :], ps[:, 1024 * t:1024 * t + 1024], ALU.add).then_inc(x_ready, 1)
                n["y"] += 1
                n["x"] += 2

            def add_y2(s):
                tt = s["tt"]
                mean_square(0)
                for st in range(tt // 2):
                    rstd_wait()
                    for t in (2 * st, 2 * st + 1):
                        ins = nc.vector.scalar_tensor_tensor(rows[:, t, :], ps[:, 1024 * t:1024 * t + 1024], rstd[:, t:t + 1],
                                                             grow[:, st, :], ALU.mult, ALU.mult)
                        if t % 2 == 0:
                            ins.then_inc(dve_link, 1)
                            n["link"] += 1
                        else:
                            link(ins)
                    if st == 0 and tt == 4:
                        mean_square(1)
                    for t in (2 * st, 2 * st + 1):
                        nc.vector.tensor_tensor(x[:, t, :], x[:, t, :], rows[:, t, :], ALU.add).then_inc(x_ready, 1)
                n["x"] += tt

            def retention_and_stick(s):
                l = s["l"]
                scale = float(P) ** -0.5

                def stick_scores(p):
                    dve.wait_ge(z_ready, 8 * l + p + 1)
                    nc.vector.tensor_scalar(zs[:, p, :], bank(2 + p % 2, 0, 384), scale, None, ALU.mult).then_inc(z_taken, 1)

                def decay(h):
                    g = 8 * l + h
                    dve.wait_ge(z_ready, g + 4 + 1)
                    if g >= 4:
                        dve.wait_ge(v_ready, g - 3)
                    nc.vector.tensor_tensor(wts[:, h, :], bank(2 + h % 2, 0, 384), rmask[:, h, :], ALU.mult).then_inc(z_taken, 1)

                def log_keep(p):
                    dve.wait_ge(l_ready, 4 * l + p + 1)
                    dve.wait_ge(z_taken, 8 * l + p + 1)
                    zz, e = zs[:, p, :], es[:, p, :]
                    link(nc.vector.scalar_tensor_tensor(e, zz, 0.0, e, ALU.max, ALU.add))
                    nc.vector.scalar_tensor_tensor(e, future[:, :], 1.0, e, ALU.subtract, ALU.mult).then_inc(lm_ready, 1)
                    nc.vector.scalar_tensor_tensor(zz, future[:, :], NEG, zz, ALU.mult, ALU.add).then_inc(dve_link, 1)
                    n["link"] += 1
                    n["z", p] = n["link"]

                def exponent(p):
                    dve.wait_ge(s_ready, 4 * l + p + 1)
                    dve.wait_ge(dve_link, n["z", p])
                    nc.vector.tensor_tensor(zs[:, p, :], zs[:, p, :], bank(6 + p % 2, 0, 384), ALU.add).then_inc(exponent_ready, 1)

                def place(h, t):
                    return 8 * (h // 4) + 4 * t + h % 4

                def head_stats(h):
                    dve.wait_ge(o_copied, 8 * l + h + 1)
                    for t in range(2):
                        last = nc.vector.bn_stats(stats[:, place(h, t), :], rows[:, t, P * h:P * h + P])
                    last.then_inc(dve_link, 1)
                    n["link"] += 1

                def variances(h0):
                    dve.wait_ge(dve_link, n["link"])
                    i0 = 2 * h0
                    for i in range(i0, i0 + 8):
                        last = nc.vector.bn_aggr(mv[:, i, :], stats[:, i, :])
                    link(last)
                    m_, mean, var = ms[:, i0:i0 + 8], mv[:, i0:i0 + 8, 0], mv[:, i0:i0 + 8, 1]
                    if h0 == 0:
                        nc.vector.tensor_scalar(m_, var, EPS, None, ALU.add).then_inc(ms_ready, 1)
                        return
                    link(nc.vector.tensor_tensor(m_, mean, mean, ALU.mult))
                    nc.vector.scalar_tensor_tensor(m_, m_, EPS, var, ALU.add, ALU.add).then_inc(ms_ready, 1)

                def normed(h0, t):
                    for h in range(h0, h0 + 4):
                        r, i = rows[:, t, P * h:P * h + P], place(h, t)
                        if h0 == 0:
                            last = nc.vector.tensor_scalar(r, r, mv[:, i, 0:1], rstd[:, i:i + 1], ALU.subtract, ALU.mult)
                        else:
                            last = nc.vector.tensor_scalar(r, r, rstd[:, i:i + 1], None, ALU.mult)
                    return last

                for p in range(4):
                    stick_scores(p)
                decay(0)
                decay(1)
                log_keep(0)
                log_keep(1)
                decay(2)
                decay(3)
                log_keep(2)
                exponent(0)
                log_keep(3)
                exponent(1)
                head_stats(0)
                head_stats(1)
                exponent(2)
                exponent(3)
                head_stats(2)
                head_stats(3)
                variances(0)
                head_stats(4)
                head_stats(5)
                rstd_wait()
                dve.wait_ge(rg_done, 2 * l + 2)
                for t in range(2):
                    link(normed(0, t))
                    nc.vector.tensor_tensor(rows[:, t, 0:512], rows[:, t, 0:512], proj1[:, t, RG:RG + 512], ALU.mult)
                head_stats(6)
                head_stats(7)
                variances(4)
                split_output_weights(s)
                rstd_wait()
                for t in range(2):
                    normed(4, t).then_inc(mix_ready, 1)
                mix_out(s, mixT1)

            def split_output_weights(s):
                for j in range(SPLIT_BEFORE):
                    split_lo(s, "u_tall", j, 0)

            def mix_out(s, dst):
                if s["kind"] == "mix":
                    dve.wait_ge(grow_ready, n["g"])
                for st in range(s["tt"] // 2):
                    for pair in (0, 2):
                        dve.wait_ge(tr_ready, n["tr"] + 4 * st + pair + 1)
                        for kk in range(2):
                            k = 2 * pair + kk
                            col = cols[:, c_mix1(s["l"]), k:k + 1] if s["kind"] == "ret" else mixcol[:, k:k + 1]
                            last = nc.vector.tensor_scalar(dst[:, k, 256 * st:256 * st + 256],
                                                           bank(4 * st + pair, 256 * kk, 256 * kk + 256), col, None, ALU.mult)
                        last.then_inc(mixT_dve, 1)
                n["tr"] += 2 * s["tt"]
                n["mixT"] += s["tt"]
                dve.wait_ge(mixT_dve, n["mixT"])
                dve.wait_ge(mixT_act, n["mixT"])

            def gmlp_norm(s):
                tt = s["tt"]
                dve.wait_ge(chunk_taken, LEAD + taken(s, 1))
                for t in range(tt):
                    link(nc.vector.tensor_tensor(vsq[:, t, :], proj2[:, t, 256:512], proj2[:, t, 256:512], ALU.mult))
                    link(nc.vector.tensor_reduce(ms[:, 4 * t:4 * t + 4], vsq[:, t, :].rearrange("p (h c) -> p h c", h=4),
                                                 AX_X, ALU.add))
                nc.vector.tensor_scalar(ms[:, 0:4 * tt], ms[:, 0:4 * tt], 1.0 / 64, EPS, ALU.mult, ALU.add).then_inc(ms_ready, 1)

            def gmlp_scale(s):
                l, tt = s["l"], s["tt"]
                rstd_wait()
                for t in range(tt):
                    for h in range(4):
                        v = proj2[:, t, 256 + 64 * h:256 + 64 * h + 64]
                        last = nc.vector.scalar_tensor_tensor(v, v, rstd[:, 4 * t + h:4 * t + h + 1],
                                                              vgain[:, l, 64 * h:64 * h + 64], ALU.mult, ALU.mult)
                    last.then_inc(v_scaled, 1)

            def mixer2(s):
                l, tt = s["l"], s["tt"]
                dve.wait_ge(ws_landed, 32 * (l + 1))
                jobs = jobs_of(s)
                scale = 64 ** -0.5
                for t in range(tt):
                    dve.wait_ge(mixed_ready, n["mixed"] + t + 1)
                    for h in range(4):
                        last = nc.vector.scalar_tensor_tensor(rows[:, t, 64 * h:64 * h + 64], bank(t, 64 * h, 64 * h + 64),
                                                              bcol[:, l, h:h + 1], proj2[:, t, 64 * h:64 * h + 64],
                                                              ALU.add, ALU.mult)
                    last.then_inc(o_copied, 1)
                n["mixed"] += tt

                def maxima(j):
                    kind, hg, m, t = jobs[j]
                    dve.wait_ge(z_ready, HEADS * DEPTH + n["job"] + j + 1)
                    b, w = 2 * (j % 2), 512 if t < 2 else 256
                    if kind == "C" and t < 2:
                        link(nc.vector.tensor_tensor(bank(b, 0, 256), bank(b, 0, 256), wmask[:, t, :], ALU.add))
                    for i in range(2 if kind == "B" else 1):
                        last = nc.vector.reduce_max(mx[:, j % 2, i:i + 1], bank(b + i, 0, w), AX_X)
                    link(last)
                    if kind == "B":
                        nc.vector.tensor_scalar(nb[:, j % 3, :], mx[:, j % 2, :], -scale, None, ALU.mult).then_inc(max_ready, 1)
                    else:
                        head = 2 * m + (hg - 4)
                        nc.vector.tensor_scalar(nb[:, j % 3, 0:1], mx[:, j % 2, 0:1], -scale, nsink[:, l, head:head + 1],
                                                ALU.mult, ALU.min).then_inc(max_ready, 1)

                def weights(j):
                    kind, hg, m, t = jobs[j]
                    dve.wait_ge(exp_ready, n["job"] + j + 1)
                    slot, w = j % 3, 512 if t < 2 else 256
                    p0, p1 = prob[:, slot, 0, 0:w], prob[:, slot, 1, 0:w]
                    if kind == "B":
                        link(nc.vector.reciprocal(rden[:, :], den[:, slot, :]))
                        link(nc.vector.tensor_scalar(rden[:, 1:2], rden[:, 1:2], nlam[:, l:l + 1], None, ALU.mult))
                        link(nc.vector.tensor_scalar(p1, p1, rden[:, 1:2], None, ALU.mult))
                        nc.vector.scalar_tensor_tensor(p0, p0, rden[:, 0:1], p1, ALU.mult, ALU.add).then_inc(prob_ready, 1)
                    else:
                        link(nc.vector.tensor_tensor(den[:, slot, 0:1], den[:, slot, 0:1], esink[:, slot:slot + 1], ALU.add))
                        link(nc.vector.reciprocal(rden[:, 0:1], den[:, slot, 0:1]))
                        nc.vector.tensor_scalar(p0, p0, rden[:, 0:1], None, ALU.mult).then_inc(prob_ready, 1)

                def output(j):
                    kind, hg, m, t = jobs[j]
                    dve.wait_ge(v_ready, HEADS * DEPTH + n["job"] + j + 1)
                    c0, w = (256 + P * hg, P) if kind == "B" else (768 + 64 * (2 * m + hg - 4), 64)
                    nc.vector.tensor_copy(rows[:, t, c0:c0 + w], bank(7, 0, w)).then_inc(o_copied, 1)
                    n["o"] = HEADS * DEPTH

                def copied(j):
                    dve.wait_ge(o_copied, HEADS * DEPTH + n["job"] + n["oa"] + tt + j + 1)

                def differential_norm(j):
                    after = j - 4 * tt
                    if 1 <= j <= 4 * tt:
                        copied(j - 1)
                        _, h, _, t = jobs[j - 1]
                        nc.vector.bn_stats(stats[:, 4 * t + h, :], rows[:, t, 256 + P * h:256 + P * h + P]).then_inc(dve_link, 1)
                        n["link"] += 1
                    if after == 1:
                        dve.wait_ge(dve_link, n["link"])
                        for i in range(4 * tt):
                            last = nc.vector.bn_aggr(mv[:, i, :], stats[:, i, :])
                        link(last)
                    if after == 2:
                        m_ = ms[:, 0:4 * tt]
                        link(nc.vector.tensor_tensor(m_, mv[:, 0:4 * tt, 0], mv[:, 0:4 * tt, 0], ALU.mult))
                        nc.vector.scalar_tensor_tensor(m_, m_, EPS, mv[:, 0:4 * tt, 1], ALU.add, ALU.add).then_inc(ms_ready, 1)
                    if after == 5:
                        rstd_wait()
                    if 5 <= after < 5 + tt:
                        for h in range(4):
                            t = after - 5
                            r = rows[:, t, 256 + P * h:256 + P * h + P]
                            last = nc.vector.tensor_scalar(r, r, rstd[:, 4 * t + h:4 * t + h + 1], None, ALU.mult)
                        last.then_inc(dve_link, 1)
                        n["link"] += 1

                for j in range(len(jobs) + 3):
                    if j < len(jobs):
                        maxima(j)
                    if 0 <= j - 1 < len(jobs):
                        weights(j - 1)
                    if 0 <= j - 3 < len(jobs):
                        differential_norm(j - 3)
                        output(j - 3)
                copied(len(jobs) - 1)
                dve.wait_ge(dve_link, n["link"])
                dve.sem_inc(mix_ready, tt)
                n["job"] += len(jobs)
                n["oa"] += tt
                split_output_weights(s)
                mix_out(s, mixT2)

            def sub_columns(s):
                l, j = s["l"], s["j"]
                weight = 1.0 if j == 1 else 0.5
                streams = s["tt"] // 2
                for st in range(s["tw"] // 2):
                    sc = modT[:, l, (3 * j + 1) * KD:(3 * j + 2) * KD, st]
                    last = nc.vector.scalar_tensor_tensor(acol[:, st, :], sc, 1.0, cols[:, c_pre(l, j), :], ALU.add, ALU.mult)
                for st in range(streams):
                    gt = modT[:, l, (3 * j + 2) * KD:(3 * j + 3) * KD, st]
                    last = nc.vector.scalar_tensor_tensor(gcol[:, st, :], gt, weight, post[:, c_post(l, j), :], ALU.mult, ALU.mult)
                if j == 1:
                    nc.vector.memset(mixcol[:, 0:2], 1.0)
                    nc.vector.memset(mixcol[:, 6:8], 1.0)
                    for k in range(2, 6):
                        last = nc.vector.tensor_scalar(mixcol[:, k:k + 1], cols[:, 13 + l, 0:1], 1.0 - LAM_INIT[l], None, ALU.mult)
                last.then_inc(cols_ready, 1)

            dve.sem_inc(gate_done, LEAD)
            dve.sem_inc(mod_taken, 1)
            dve.sem_inc(mod_rows, 2)
            dve.sem_inc(mod_split, LEAD)
            nc.vector.memset(cstat[:, :, :].bitcast(F32), 0.0).then_inc(dve_link, 1)
            n["link"] += 1
            nc.vector.memset(ones[:, :], 1.0)
            nc.vector.memset(zero[:, :], 0.0)
            link(nc.vector.memset(mhalf[:, :], -0.5))
            dve.wait_ge(consts_landed, 16 * n_consts)
            link(nc.vector.tensor_tensor(lprod[:, :, :, :], lamw[:, :, 0:4:2, :], lamw[:, :, 1:4:2, :], ALU.mult))
            nc.vector.tensor_reduce(lsum[:, :, :], lprod[:, :, :, :], AX_X, ALU.add).then_inc(lam_ready, 1)
            dve.wait_ge(c_silu, 1)
            link(nc.vector.tensor_copy(cstat[:, :, 0:2], cT[:, :, :]))
            nc.vector.tensor_tensor(cstat[:, :, 2:4], cT[:, :, :], cstat[:, :, 0:2].bitcast(F32), ALU.subtract)
            nc.vector.tensor_tensor(sel[:, :], ident[:, 0:2], ident[:, 2:4], ALU.add).then_inc(c_split, 1)
            link(nc.vector.tensor_scalar(nsink[:, :, :], sink[:, :, :], -1.0, None, ALU.mult))
            dve.wait_ge(lexp_ready, 1)
            link(nc.vector.tensor_tensor(nlam[:, :], lsum[:, :, 1], lsum[:, :, 0], ALU.subtract))
            for l in range(DEPTH):
                link(nc.vector.tensor_scalar(nlam[:, l:l + 1], nlam[:, l:l + 1], -LAM_INIT[l], None, ALU.add))
            dve.wait_ge(x_landed, 16)
            for i, s in enumerate(SUBS):
                if i == 2 * DEPTH:
                    mean_square(0)
                    rstd_wait()
                    dve.wait_ge(grow_ready, 1)
                    n["g"] += 1
                    for t in range(2):
                        nc.vector.scalar_tensor_tensor(x[:, t, :], x[:, t, :], rstd[:, t:t + 1], grow[:, 0, :],
                                                       ALU.mult, ALU.mult).then_inc(x_ready, 1)
                    n["x"] += 2
                if i:
                    dve.wait_ge(x_ready, n["x"])
                if s["blk"] == 2:
                    n["g"] += s["tt"] // 2
                    dve.wait_ge(cols_ready, 2 + i - 2 * DEPTH)
                if s["blk"] == 1 and rows_wanted(s)[0]:
                    nc.vector.tensor_copy(gcol[:, 0, :], cols[:, C_FINAL, :]).then_inc(cols_ready, 1)
                norm_rows(s["tw"])
                for u in range(3 if i == 0 else 0):
                    split_lo(s, "u_wide", u, 0)
                split_rows(s)
                if i == 0:
                    dve.wait_ge(late_landed, 16 * n_late)
                wide(s)
                if s["kind"] == "ret":
                    retention_and_stick(s)
                if s["kind"] == "mix":
                    mixer2(s)
                if s["kind"] == "ffn":
                    dve.wait_ge(chunk_taken, taken_total(s))
                tall(s)
                if i + 1 < len(SUBS):
                    for u in range(3):
                        split_lo(SUBS[i + 1], "u_wide", u, 0)
                    if SUBS[i + 1]["blk"] == 2:
                        dve.wait_ge(diag_ready, n["g"] + (i == 2 * DEPTH - 1))
                        sub_columns(SUBS[i + 1])
                if s["blk"] == 1:
                    add_y1(s)
                else:
                    dve.wait_ge(grow_ready, n["g"])
                    add_y2(s)

        @block.gpsimd
        def _(pool):
            n = Counter()

            def link(ins):
                n["link"] += 1
                ins.then_inc(pool_link, 1)
                pool.wait_ge(pool_link, n["link"])

            def inverse_root(m, m0=0):
                n["ms"] += 1
                pool.wait_ge(ms_ready, n["ms"])
                nc.gpsimd.tensor_tensor(rstd[:, m0:m], ms[:, m0:m], mhalf[:, m0:m], ALU.pow).then_inc(rstd_ready, 1)

            def inverse_roots(tiles):
                for st in range(tiles // 2):
                    inverse_root(2 * st + 2, 2 * st)

            def diagonals(s):
                streams, _, diag = rows_wanted(s)
                if not streams:
                    return
                n["cols"] += 1
                pool.wait_ge(cols_ready, n["cols"])
                if s["blk"] == 1:
                    pool.wait_ge(w_used, LEAD + s["u_wide"] + 1)
                for st in range(streams):
                    for k in range(KD):
                        last = nc.gpsimd.tensor_scalar(diag[:, st, k, :], ident[:, :], gcol[:, st, k:k + 1], None, ALU.mult)
                    last.then_inc(diag_ready, 1)

            def rope(view, cos, tmp, swap):
                t1, t2 = tmp
                link(nc.gpsimd.tensor_tensor(t1, view, cos, ALU.mult))
                for dst, src, sn in swap:
                    last = nc.gpsimd.tensor_tensor(dst, src, sn, ALU.mult)
                link(last)
                link(nc.gpsimd.tensor_tensor(view, t1, t2, ALU.add))

            def rope_first(s):
                pool.wait_ge(late_landed, 16 * n_late)
                pool.wait_ge(chunk_taken, LEAD + s["take0"] + 4)
                for t in range(2):
                    v = proj1[:, t, 0:D]
                    t1, t2 = rope1[:, 0, :], rope1[:, 1, :]
                    v8, t18, t28 = (q.rearrange("p (h c) -> p h c", h=8) for q in (v, t1, t2))
                    cos = cs1[:, t, 0, :].unsqueeze(1).broadcast_to([P, 8, P])
                    sins = [cs1[:, t, 1, 64 * i:64 * i + 64].unsqueeze(1).broadcast_to([P, 8, 64]) for i in range(2)]
                    swap = [(t28[:, :, 64 * i:64 * i + 64], v8[:, :, 64 - 64 * i:128 - 64 * i], sins[i]) for i in range(2)]
                    rope(v8, cos, (t18, t28), swap)
                    pool.sem_inc(rope_done, 1)

            def rope_second(s):
                for c0, w in ((QB, 512), (QC, 256), (KB, 512), (KC, 128)):
                    pool.wait_ge(chunk_taken, LEAD + taken(s, (c0 + w - 1) // CH + 1))
                    if c0 == QC:
                        inverse_root(4 * s["tt"])
                    for t in range(2):
                        g = w // 64
                        v, t1, t2 = proj2[:, t, c0:c0 + w], rope2[:, 0, 0:w], rope2[:, 1, 0:w]
                        v8, t18 = (q.rearrange("p (h c) -> p h c", h=g) for q in (v, t1))
                        cos = cs2[:, t, 0, :].unsqueeze(1).broadcast_to([P, g, 64])
                        swap = []
                        v5, t5 = (q.rearrange("p (h a b c) -> p h a b c", h=g, a=2, b=2) for q in (v, t2))
                        s5 = cs2[:, t, 1, :].rearrange("p (a b c) -> p a b c", a=2, b=2)
                        for b in range(2):
                            swap.append((t5[:, :, :, b, :], v5[:, :, :, 1 - b, :],
                                         s5[:, :, b, :].unsqueeze(1).broadcast_to([P, g, 2, 16])))
                        t28 = t2.rearrange("p (h c) -> p h c", h=g)
                        rope(v8, cos, (t18, t28), swap)
                        pool.sem_inc(rope_done, 1)

            pool.wait_ge(dve_link, 2)
            pool.wait_ge(consts_landed, 16 * n_consts)
            for i, s in enumerate(SUBS):
                if i == 2 * DEPTH:
                    inverse_root(2)
                inverse_roots(s["tw"])
                diagonals(s)
                if s["kind"] == "ret":
                    rope_first(s)
                    inverse_root(8)
                    inverse_root(16, 8)
                if s["kind"] == "mix":
                    pool.dma_start(ws[:, :, :], a["ws"][s["l"]]).then_inc(ws_landed, 16)
                    pool.dma_start(wmask[:, :, :], a["wmask"]).then_inc(ws_landed, 16)
                    rope_second(s)
                    inverse_root(4 * s["tt"])
                if s["blk"] == 2:
                    inverse_roots(s["tt"])


def shape_constants():
    import numpy as np
    f = np.float32
    c = {"ident": np.eye(P, dtype=f)}
    pos = np.arange(256, dtype=f)
    inv = (1.0 / (f(ROPE_BASE) ** (np.arange(0, P, 2, dtype=f) / f(P)))).astype(f)
    ang = pos[:, None] * inv[None, :]
    cos, sin = np.cos(ang), np.sin(ang)
    cs = np.stack([np.concatenate([cos, cos], 1), np.concatenate([-sin, sin], 1)], 1)
    c["cs1"] = cs.reshape(2, P, 2, P).transpose(1, 0, 2, 3)
    row, col = np.repeat(np.arange(4, dtype=f), GRID_W), np.tile(np.arange(GRID_W, dtype=f), 4)
    inv = (f(ROPE_BASE) ** (-np.arange(16, dtype=f) / f(16))).astype(f)
    ar, ac = row[:, None] * inv, col[:, None] * inv
    cos = np.concatenate([np.cos(ar)] * 2 + [np.cos(ac)] * 2, 1)
    sin = np.concatenate([-np.sin(ar), np.sin(ar), -np.sin(ac), np.sin(ac)], 1)
    c["cs2"] = np.stack([cos, sin], 1).reshape(2, P, 2, 64).transpose(1, 0, 2, 3)
    s_, t_ = np.arange(P)[:, None], np.arange(P)[None, :]
    diag = (s_ < t_).astype(f)
    valid = np.concatenate([diag, np.ones((P, P), f), diag], 1)
    c["future"] = 1.0 - valid
    c["tri"] = (s_ >= t_).astype(f)
    heads = []
    for h in range(4):
        log_g = np.log1p(-np.exp2(-5.0 - h))
        parts = []
        for sk, tq in ((0, 0), (0, 1), (1, 1)):
            s, t = s_ + P * sk, t_ + P * tq
            w = np.exp(log_g * np.abs(t - s)) * ((s // CHUNK) <= (t // CHUNK)) * P ** -0.5
            parts.append(w)
        heads.append(np.concatenate(parts, 1))
    c["rmask"] = np.stack(heads, 1).astype(f)
    q = np.arange(256).reshape(2, P)
    keys = np.arange(256)
    c["wmask"] = np.stack([np.where(np.abs(q[t][:, None] - keys[None, :]) <= WINDOW, 0.0, NEG) for t in range(2)], 1).astype(f)
    return {k: np.ascontiguousarray(v.astype(f)) for k, v in c.items()}


def kernel(**inputs):
    import numpy as np
    import concourse.bacc as bacc
    from concourse.bass_utils import run_bass_kernel_spmd

    v = {k: np.asarray(a) for k, a in inputs.items()}
    order = np.arange(2560)
    order[QC:QC + 256] = QC + np.arange(256).reshape(2, 2, 64).transpose(1, 0, 2).reshape(-1)

    def wide_units(*mats):
        w = CH // len(mats)
        m = [a.reshape(KD, P, -1, w) for a in mats]
        m = np.stack(m, 3)
        m = m.reshape(4, 2, P, -1, CH).transpose(3, 0, 2, 1, 4)
        return m.reshape(-1, P, UNIT)

    def tall_units(a):
        return a.reshape(-1, P, D)

    units = []
    for l in range(DEPTH):
        units += [wide_units(v["w_in"][l]), tall_units(v["w_out"][l]),
                  wide_units(v["w_gate"][l], v["w_up"][l]), tall_units(v["w_down"][l])]
    for l in range(DEPTH):
        g, u, d = v["ffn_w_gate_2"][l], v["ffn_w_up_2"][l], v["ffn_w_down_2"][l]
        units += [wide_units(g[0], u[0]), tall_units(d[0]),
                  wide_units(v["w_in_2"][l][:, order]), tall_units(v["w_out_2"][l]),
                  wide_units(g[1], u[1]), tall_units(d[1])]

    def column(a):
        return a.reshape(-1, P).T

    subln = [np.stack([v["diff_subln_2"][l]] + [v["diff_subln_2"][l]] * (KD - 1), 1) for l in range(DEPTH)]
    cols = ([column(v["norm1_g"][l]) for l in range(DEPTH)] + [column(v["norm2_g"][l]) for l in range(DEPTH)]
            + [column(np.concatenate([v["ret_norm_g"][l], v["sb_norm_g"][l]])) for l in range(DEPTH)]
            + [column(v["final_g"])]
            + [column(v["norm_pre_2"][l, j]) for l in range(DEPTH) for j in range(3)] + subln)
    arrays = dict(
        x=v["x"], ctx=v["ctx_2"],
        w=np.concatenate(units, 0),
        w_mod=np.concatenate([wide_units(v["w_mod_2"][l]) for l in range(DEPTH)], 0),
        cols=np.stack(cols, 1),
        post=np.stack([column(v["norm_post_2"][l, j]) for l in range(DEPTH) for j in range(3)], 1),
        bmod=np.stack([column(v["b_mod_2"][l]) for l in range(DEPTH)], 1),
        cT=np.stack([column(v["c_2"][0]), column(v["c_ctx_2"])], 2),
        bcol=v["gmlp_b_s_2"].transpose(2, 0, 1),
        ws=v["gmlp_w_s_2"].transpose(0, 3, 1, 2),
        vgain=v["gmlp_v_gain_2"].reshape(DEPTH, 256),
        lam=v["diff_lambda_2"], sink=v["swa_sink_2"],
        **shape_constants())
    nc = bacc.Bacc("TRN2", target_bir_lowering=False, num_devices=1)
    feeds, aps = {}, {}
    for name, arr in arrays.items():
        arr = np.ascontiguousarray(arr)
        feeds["in_" + name] = arr
        aps[name] = nc.dram_tensor("in_" + name, arr.shape, mybir.dt.from_np(arr.dtype), kind="ExternalInput").ap()
    out = nc.dram_tensor("out", (1, 256, D), F32, kind="ExternalOutput").ap()
    build(nc, aps, out)
    r = run_bass_kernel_spmd(nc, [feeds], core_ids=[0])
    return r.results[0]["out"]
```
